# Optimizing a Trainium2 kernel written in Bass

```python
import math
import jax
import jax.numpy as jnp
from jax import lax
import numpy as np

D_MODEL = 1024
BATCH = 1
SEQ = 256
DEPTH = 2

CHUNK = 64
N_EVEN = (DEPTH + 1) // 2
N_ODD = DEPTH // 2
EPS = 1e-6
ADA_SCALE = 0.5

MIX_WIDTH = D_MODEL
POOL_WIDTH = MIX_WIDTH // 2
POOL_WINDOWS = (2, 4, 8, 16)
N_POOL = len(POOL_WINDOWS)
POOL_GROUP = POOL_WIDTH // N_POOL
S5_WIDTH = MIX_WIDTH - POOL_WIDTH
S5_GROUP = 16
S5_GROUPS = S5_WIDTH // S5_GROUP
S5_STATE = 64
S5_DT_MIN = 1e-3
S5_DT_MAX = 1e-1

M2_INNER = 2 * D_MODEL
M2_HEADDIM = 64
M2_HEADS = M2_INNER // M2_HEADDIM
M2_GROUPS = 8
M2_HPG = M2_HEADS // M2_GROUPS
M2_STATE = 128
M2_CONV = 4
M2_BC = M2_GROUPS * M2_STATE
M2_CONV_DIM = M2_INNER + 2 * M2_BC
M2_PROJ = M2_INNER + M2_CONV_DIM + M2_HEADS
M2_DT_MIN = 1e-3
M2_DT_MAX = 1e-1

FFN_HIDDEN = 2816
N_EXPERTS = 8
TOP_K = 2
EXPERT_HIDDEN = 3584

kernel_name = "hybrid_pool_s5_ssd_moe_streaming_trunk"

def _rmsnorm(x, g):
    xf = x.astype(jnp.float32)
    y = xf * lax.rsqrt(jnp.mean(xf * xf, axis=-1, keepdims=True) + EPS)
    return (y * g.astype(jnp.float32)).astype(x.dtype)

def _modulate(x, g, shift, scale):
    return _rmsnorm(x, g) * (1.0 + scale) + shift

def _swiglu(h, w_gate, w_up, w_down):
    return (jax.nn.silu(h @ w_gate) * (h @ w_up)) @ w_down

def _pool_mixer(u, pool_w, pool_scale):
    s = u.shape[1]
    uf = u.astype(jnp.float32)
    cs = jnp.cumsum(uf, axis=1)
    t = jnp.arange(1, s + 1, dtype=jnp.float32)
    outs = []
    for gi, win in enumerate(POOL_WINDOWS):
        sl = slice(gi * POOL_GROUP, (gi + 1) * POOL_GROUP)
        cs_g = cs[..., sl]
        lag = jnp.pad(cs_g, ((0, 0), (win, 0), (0, 0)))[:, :s]
        count = jnp.minimum(t, float(win))[None, :, None]
        pooled = (cs_g - lag) / count - uf[..., sl]
        outs.append(pooled @ pool_w[gi].astype(jnp.float32))
    return jnp.concatenate(outs, axis=-1) * pool_scale.astype(jnp.float32)

def _complex_combine(left, right):
    a1r, a1i, b1r, b1i = left
    a2r, a2i, b2r, b2i = right
    return (a2r * a1r - a2i * a1i,
            a2r * a1i + a2i * a1r,
            a2r * b1r - a2i * b1i + b2r,
            a2r * b1i + a2i * b1r + b2i)

def _s5_mixer(u, lam_re, lam_im, log_step, b_re, b_im, c_re, c_im, d_skip, w_glu):
    f32 = jnp.float32
    bsz, s, _ = u.shape
    uf = u.astype(f32).reshape(bsz, s, S5_GROUPS, S5_GROUP)
    step = jnp.exp(log_step.astype(f32))[:, None]
    lr = jnp.minimum(lam_re.astype(f32), -1e-4)
    li = lam_im.astype(f32)
    mag = jnp.exp(lr * step)
    ar = mag * jnp.cos(li * step)
    ai = mag * jnp.sin(li * step)
    inv = 1.0 / (lr * lr + li * li)
    fr = ((ar - 1.0) * lr + ai * li) * inv
    fi = (ai * lr - (ar - 1.0) * li) * inv
    br, bi = b_re.astype(f32), b_im.astype(f32)
    bbr = fr[..., None] * br - fi[..., None] * bi
    bbi = fr[..., None] * bi + fi[..., None] * br
    bu_r = jnp.einsum("bsgh,gph->sbgp", uf, bbr)
    bu_i = jnp.einsum("bsgh,gph->sbgp", uf, bbi)
    a_r = jnp.broadcast_to(ar, (s, 1) + ar.shape)
    a_i = jnp.broadcast_to(ai, (s, 1) + ai.shape)
    _, _, xr, xi = lax.associative_scan(_complex_combine, (a_r, a_i, bu_r, bu_i), axis=0)
    y = (jnp.einsum("sbgp,ghp->bsgh", xr, c_re.astype(f32))
         - jnp.einsum("sbgp,ghp->bsgh", xi, c_im.astype(f32)))
    y = y + d_skip.astype(f32).reshape(S5_GROUPS, S5_GROUP) * uf
    y = jax.nn.gelu(y.reshape(bsz, s, S5_WIDTH))
    return y * jax.nn.sigmoid(y @ w_glu.astype(f32))

def _pool_s5_block(h, w_in, pool_w, pool_scale, lam_re, lam_im, log_step,
                   b_re, b_im, c_re, c_im, s5_d, w_glu, w_out):
    u = h @ w_in
    y_pool = _pool_mixer(u[..., :POOL_WIDTH], pool_w, pool_scale)
    y_s5 = _s5_mixer(u[..., POOL_WIDTH:], lam_re, lam_im, log_step,
                     b_re, b_im, c_re, c_im, s5_d, w_glu)
    y = jnp.concatenate([y_pool, y_s5], axis=-1).astype(h.dtype)
    return y @ w_out

def _ssd_scan(xs, dt, a, bm, cm):
    bsz, s = xs.shape[:2]
    nc = s // CHUNK
    xdt = (xs * dt[..., None]).reshape(bsz, nc, CHUNK, M2_GROUPS, M2_HPG, M2_HEADDIM)
    da = (dt * a).reshape(bsz, nc, CHUNK, M2_GROUPS, M2_HPG)
    bm = bm.reshape(bsz, nc, CHUNK, M2_GROUPS, M2_STATE)
    cm = cm.reshape(bsz, nc, CHUNK, M2_GROUPS, M2_STATE)
    cs = jnp.cumsum(da, axis=2)
    causal = jnp.tril(jnp.ones((CHUNK, CHUNK), dtype=bool))[:, :, None, None]
    seg = cs[:, :, :, None] - cs[:, :, None, :]
    decay = jnp.exp(jnp.where(causal, seg, -jnp.inf))
    cb = jnp.einsum("bclgn,bcsgn->bclsg", cm, bm)
    y_diag = jnp.einsum("bclsgj,bcsgjp->bclgjp", cb[..., None] * decay, xdt)
    to_end = jnp.exp(cs[:, :, -1:] - cs)
    states = jnp.einsum("bclgn,bclgjp->bcgjpn", bm, xdt * to_end[..., None])
    chunk_decay = jnp.exp(cs[:, :, -1])

    def step(carry, inp):
        st, dec = inp
        return carry * dec[..., None, None] + st, carry

    init = jnp.zeros((bsz, M2_GROUPS, M2_HPG, M2_HEADDIM, M2_STATE), jnp.float32)
    _, prev = lax.scan(step, init, (jnp.moveaxis(states, 1, 0), jnp.moveaxis(chunk_decay, 1, 0)))
    prev = jnp.moveaxis(prev, 0, 1)
    y_off = jnp.einsum("bclgn,bcgjpn->bclgjp", cm, prev) * jnp.exp(cs)[..., None]
    return (y_diag + y_off).reshape(bsz, s, M2_HEADS, M2_HEADDIM)

def _mamba2_mixer(h, w_in, conv_w, conv_b, dt_bias, a_log, d_skip, norm_g, w_out):
    f32 = jnp.float32
    bsz, s, _ = h.shape
    proj = h @ w_in
    z = proj[..., :M2_INNER]
    xbc = proj[..., M2_INNER:M2_INNER + M2_CONV_DIM]
    dt_raw = proj[..., M2_INNER + M2_CONV_DIM:]
    xbc = lax.conv_general_dilated(
        xbc, conv_w[:, None, :], window_strides=(1,), padding=[(M2_CONV - 1, 0)],
        dimension_numbers=("NWC", "WIO", "NWC"), feature_group_count=M2_CONV_DIM)
    xbc = jax.nn.silu(xbc + conv_b).astype(f32)
    xs = xbc[..., :M2_INNER].reshape(bsz, s, M2_HEADS, M2_HEADDIM)
    bm = xbc[..., M2_INNER:M2_INNER + M2_BC].reshape(bsz, s, M2_GROUPS, M2_STATE)
    cm = xbc[..., M2_INNER + M2_BC:].reshape(bsz, s, M2_GROUPS, M2_STATE)
    dt = jax.nn.softplus(dt_raw.astype(f32) + dt_bias.astype(f32))
    a = -jnp.exp(a_log.astype(f32))
    y = _ssd_scan(xs, dt, a, bm, cm) + d_skip.astype(f32)[:, None] * xs
    y = y.reshape(bsz, s, M2_INNER) * jax.nn.silu(z.astype(f32))
    y = _rmsnorm(y, norm_g).astype(h.dtype)
    return y @ w_out

def _moe_swiglu(h, w_router, b_router, w_gate, w_up, w_down):
    bsz, s, d = h.shape
    tok = h.reshape(bsz * s, d)
    logits = (tok @ w_router).astype(jnp.float32) + b_router.astype(jnp.float32)
    top_logit, top_idx = lax.top_k(logits, TOP_K)
    top_w = jax.nn.softmax(top_logit, axis=-1)
    gates = jnp.einsum("tk,tke->te", top_w,
                       jax.nn.one_hot(top_idx, N_EXPERTS, dtype=jnp.float32))
    out = jnp.zeros((bsz * s, d), jnp.float32)
    for e in range(N_EXPERTS):
        y_e = _swiglu(tok, w_gate[e], w_up[e], w_down[e]).astype(jnp.float32)
        out = out + gates[:, e:e + 1] * y_e
    return out.astype(h.dtype).reshape(bsz, s, d)

def setup_inputs(seed: int = 0) -> dict:
    key = jax.random.key(seed)
    ks = iter(jax.random.split(key, 64))
    f32 = jnp.float32

    def nrm(shape, scale):
        return jax.random.normal(next(ks), shape, f32) * scale

    def log_uniform(shape, lo, hi):
        return jax.random.uniform(next(ks), shape, f32, math.log(lo), math.log(hi))

    ne, no = N_EVEN, N_ODD
    x = nrm((BATCH, SEQ, D_MODEL), 1.0)
    c = nrm((BATCH, D_MODEL), 1.0)
    ada_w = nrm((DEPTH, D_MODEL, 6 * D_MODEL), ADA_SCALE * D_MODEL ** -0.5)
    ada_b = nrm((DEPTH, 6 * D_MODEL), 0.02)
    norm_g = 1.0 + nrm((DEPTH, 4, D_MODEL), 0.02)
    mix_w_in = nrm((ne, D_MODEL, MIX_WIDTH), D_MODEL ** -0.5)
    pool_w = nrm((ne, N_POOL, POOL_GROUP, POOL_GROUP), POOL_GROUP ** -0.5)
    pool_scale = 1.0 + nrm((ne, POOL_WIDTH), 0.05)
    s5_lam_re = -0.5 + nrm((ne, S5_GROUPS, S5_STATE), 0.01)
    s5_lam_im = math.pi * jnp.arange(S5_STATE, dtype=f32) + nrm((ne, S5_GROUPS, S5_STATE), 0.01)
    s5_log_step = log_uniform((ne, S5_GROUPS), S5_DT_MIN, S5_DT_MAX)
    s5_b_re = nrm((ne, S5_GROUPS, S5_STATE, S5_GROUP), (2.0 * S5_GROUP) ** -0.5)
    s5_b_im = nrm((ne, S5_GROUPS, S5_STATE, S5_GROUP), (2.0 * S5_GROUP) ** -0.5)
    s5_c_re = nrm((ne, S5_GROUPS, S5_GROUP, S5_STATE), 0.5 ** 0.5)
    s5_c_im = nrm((ne, S5_GROUPS, S5_GROUP, S5_STATE), 0.5 ** 0.5)
    s5_d = nrm((ne, S5_WIDTH), 0.5)
    s5_w_glu = nrm((ne, S5_WIDTH, S5_WIDTH), S5_WIDTH ** -0.5)
    mix_w_out = nrm((ne, MIX_WIDTH, D_MODEL), MIX_WIDTH ** -0.5)
    ffn_w_gate = nrm((ne, D_MODEL, FFN_HIDDEN), D_MODEL ** -0.5)
    ffn_w_up = nrm((ne, D_MODEL, FFN_HIDDEN), D_MODEL ** -0.5)
    ffn_w_down = nrm((ne, FFN_HIDDEN, D_MODEL), FFN_HIDDEN ** -0.5)
    m2_w_in = nrm((no, D_MODEL, M2_PROJ), D_MODEL ** -0.5)
    m2_conv_w = nrm((no, M2_CONV, M2_CONV_DIM), M2_CONV ** -0.5)
    m2_conv_b = nrm((no, M2_CONV_DIM), 0.02)
    dt0 = jnp.exp(log_uniform((no, M2_HEADS), M2_DT_MIN, M2_DT_MAX))
    m2_dt_bias = dt0 + jnp.log(-jnp.expm1(-dt0))
    m2_a_log = jnp.log(jax.random.uniform(next(ks), (no, M2_HEADS), f32, 1.0, 16.0))
    m2_d = 1.0 + nrm((no, M2_HEADS), 0.1)
    m2_norm_g = 1.0 + nrm((no, M2_INNER), 0.02)
    m2_w_out = nrm((no, M2_INNER, D_MODEL), M2_INNER ** -0.5)
    moe_w_router = nrm((no, D_MODEL, N_EXPERTS), D_MODEL ** -0.5)
    moe_b_router = nrm((no, N_EXPERTS), 0.01)
    moe_w_gate = nrm((no, N_EXPERTS, D_MODEL, EXPERT_HIDDEN), D_MODEL ** -0.5)
    moe_w_up = nrm((no, N_EXPERTS, D_MODEL, EXPERT_HIDDEN), D_MODEL ** -0.5)
    moe_w_down = nrm((no, N_EXPERTS, EXPERT_HIDDEN, D_MODEL), EXPERT_HIDDEN ** -0.5)
    return {
        "x": x, "c": c, "ada_w": ada_w, "ada_b": ada_b, "norm_g": norm_g,
        "mix_w_in": mix_w_in, "pool_w": pool_w, "pool_scale": pool_scale,
        "s5_lam_re": s5_lam_re, "s5_lam_im": s5_lam_im, "s5_log_step": s5_log_step,
        "s5_b_re": s5_b_re, "s5_b_im": s5_b_im, "s5_c_re": s5_c_re, "s5_c_im": s5_c_im,
        "s5_d": s5_d, "s5_w_glu": s5_w_glu, "mix_w_out": mix_w_out,
        "ffn_w_gate": ffn_w_gate, "ffn_w_up": ffn_w_up, "ffn_w_down": ffn_w_down,
        "m2_w_in": m2_w_in, "m2_conv_w": m2_conv_w, "m2_conv_b": m2_conv_b,
        "m2_dt_bias": m2_dt_bias, "m2_a_log": m2_a_log, "m2_d": m2_d,
        "m2_norm_g": m2_norm_g, "m2_w_out": m2_w_out,
        "moe_w_router": moe_w_router, "moe_b_router": moe_b_router,
        "moe_w_gate": moe_w_gate, "moe_w_up": moe_w_up, "moe_w_down": moe_w_down,
    }

def reference(x, c, ada_w, ada_b, norm_g, mix_w_in, pool_w, pool_scale,
              s5_lam_re, s5_lam_im, s5_log_step, s5_b_re, s5_b_im, s5_c_re, s5_c_im,
              s5_d, s5_w_glu, mix_w_out, ffn_w_gate, ffn_w_up, ffn_w_down,
              m2_w_in, m2_conv_w, m2_conv_b, m2_dt_bias, m2_a_log, m2_d,
              m2_norm_g, m2_w_out, moe_w_router, moe_b_router,
              moe_w_gate, moe_w_up, moe_w_down):
    for layer in range(DEPTH):
        i = layer // 2
        mod = (jax.nn.silu(c) @ ada_w[layer] + ada_b[layer])[:, None, :]
        sh_m, sc_m, g_m, sh_f, sc_f, g_f = jnp.split(mod, 6, axis=-1)
        h = _modulate(x, norm_g[layer, 0], sh_m, sc_m)
        if layer % 2 == 0:
            y = _pool_s5_block(h, mix_w_in[i], pool_w[i], pool_scale[i],
                               s5_lam_re[i], s5_lam_im[i], s5_log_step[i],
                               s5_b_re[i], s5_b_im[i], s5_c_re[i], s5_c_im[i],
                               s5_d[i], s5_w_glu[i], mix_w_out[i])
        else:
            y = _mamba2_mixer(h, m2_w_in[i], m2_conv_w[i], m2_conv_b[i], m2_dt_bias[i],
                              m2_a_log[i], m2_d[i], m2_norm_g[i], m2_w_out[i])
        x = x + g_m * _rmsnorm(y, norm_g[layer, 1])
        h = _modulate(x, norm_g[layer, 2], sh_f, sc_f)
        if layer % 2 == 0:
            y = _swiglu(h, ffn_w_gate[i], ffn_w_up[i], ffn_w_down[i])
        else:
            y = _moe_swiglu(h, moe_w_router[i], moe_b_router[i],
                            moe_w_gate[i], moe_w_up[i], moe_w_down[i])
        x = x + g_f * _rmsnorm(y, norm_g[layer, 3])
    return x


_drawn_inputs = setup_inputs


def setup_inputs(seed=0):
    import zlib

    import numpy as np

    out = dict(_drawn_inputs(seed))
    spreads = {}
    factors = {'s5_lam_re': 8.0, 'm2_conv_b': 4.368, 'm2_norm_g': 3.454, 'moe_b_router': 3.311}
    for name, (base, spread) in spreads.items():
        noise = np.random.default_rng([zlib.crc32(name.encode()), seed]).standard_normal(out[name].shape)
        drawn = base * np.exp(spread * noise) if base else spread * noise
        out[name] = jnp.asarray(drawn.astype(out[name].dtype))
    for name, factor in factors.items():
        out[name] = (out[name] * factor).astype(out[name].dtype)
    return out
```

```python
from contextlib import ExitStack

import concourse.bass as bass
from concourse import mybir

ALU = mybir.AluOpType
ACT = mybir.ActivationFunctionType
AX = mybir.AxisListType
F32 = mybir.dt.float32
I32 = mybir.dt.int32

P = 128
D = 1024
KC = D // P
TOK = 256
NB = TOK // P
EPS = 1e-6
HALF = 512
NADA = 6 * D // HALF
POOL_WINDOWS = (2, 4, 8, 16)
NQ = 16
FFN = 2816
INNER = 2048
HEADS = 32
NG = 8
NE = 8
EH = 3584
RING = 7
TILE = 4096
S5_SLOTS = 4
L1_SLOTS = 6
ROUND = 12582912.0
TWO_PI = 6.283185
INV_TWO_PI = 0.15915494309189535
WIDTHS = (512, 512, 512, 256)
ITEM = 21


def plan():
    tiles = []

    def put(kind, n, slot):
        tiles.append((kind, n, slot))

    head = [("ada0", n) for n in range(4)] + [("mixin", 0), ("mixin", 1)]
    head += [("ada0", n) for n in range(4, NADA)] + [("glu", 0), ("mixout", 0), ("mixout", 1)]
    for n, (kind, i) in enumerate(head):
        put(kind, i, n % S5_SLOTS)
    ffn, ada = [], [("ada1", n) for n in range(NADA)]
    for t in range(6):
        ffn += [("gate", t), ("up", t), ada[2 * t]]
        if t:
            ffn.append(("down", t - 1))
        ffn.append(ada[2 * t + 1])
    ffn.append(("down", 5))
    for n, (kind, i) in enumerate(ffn):
        put(kind, i, (n + 4) % RING)
    l1 = [("xbc", n) for n in range(8)] + [("z", n) for n in range(4)] + [("m2out", n) for n in range(4)]
    for n, (kind, i) in enumerate(l1):
        put(kind, i, (n - len(l1)) % L1_SLOTS)
    return tiles


TILES = plan()
NTILES = len(TILES)
AT = {(kind, n): i for i, (kind, n, _) in enumerate(TILES)}
ADA = [AT[f"ada{i // NADA}", i % NADA] for i in range(2 * NADA)]
LAST_SLOT6 = max(i for i, t in enumerate(TILES) if t[2] == 6)
MOE0 = NTILES + 1
FILL, LAST_USER = [], []
_fills, _user = [0] * RING, [None] * RING
for _i, (_k, _n, _s) in enumerate(TILES):
    _fills[_s] += 1
    FILL.append(_fills[_s])
    LAST_USER.append(_user[_s])
    _user[_s] = _i
FILLS0 = list(_fills)
ORDER = []
for _t in range(4):
    _m = 2 if _t < 3 else 1
    ORDER += [("g", _t, _m), ("u", _t, _m)] + ([("d", _t - 1, 2)] if _t else [])
ORDER.append(("d", 3, 1))
FIRST, DONE = {}, {}
_at = 0
for _w, _t, _m in ORDER:
    FIRST[_w, _t] = _at
    _at += _m
    DONE[_w, _t] = _at
assert _at == ITEM and ITEM % RING == 0


def hybrid_trunk(nc, a, out):
    with ExitStack() as ctx:
        def sb(name, shape, dt=F32):
            return ctx.enter_context(nc.sbuf_tensor(name, shape, dt))

        def sem(name):
            return ctx.enter_context(nc.semaphore(name))

        ps = [ctx.enter_context(nc.psum_tensor(f"bank{i}", [P, HALF], F32)) for i in range(8)]

        ring = sb("ring", [P, RING, TILE])
        x = sb("x", [P, NB, D])
        ident = sb("ident", [P, P])
        tri = sb("tri", [P, P])
        ntri = sb("ntri", [P, P])
        after = sb("after", [P, P])
        ones = sb("ones", [P, P])
        slot_iota = sb("slot_iota", [P, P])
        earlier = sb("earlier", [P, NE, NE])
        cols = sb("cols", [P, 3, P])
        mod = sb("mod", [P, 2, 6, KC])
        mod_flat = mod[:, :, :, :].rearrange("p l v k -> p (l v k)")
        modraw = sb("modraw", [P, 2, 4])
        cT = sb("cT", [P, KC, 32])
        gs = sb("gs", [P, KC])
        gg = sb("gg", [P, KC])
        stat = sb("stat", [P, 16])
        rst = sb("rst", [P, 10])
        s5_tmp = sb("s5_tmp", [P, NQ, 16])
        eps = sb("eps", [P, 1])
        dtw = sb("dtw", [P, KC, HEADS])
        rw = sb("rw", [P, KC, NE])
        bro = sb("bro", [P, 3 * HEADS + NE])
        hd = sb("hd", [P, 6, NB, HEADS])
        rt = sb("rt", [P, 6, NB, NE])
        pair = sb("pair", [P, 2, NE * NE])
        cnt_f = sb("cnt_f", [1, 17])
        cnt = sb("cnt", [1, 17], I32)
        ARENA = 19456
        arena = sb("arena", [P, ARENA])

        def area(at, *shape):
            n = 1
            for s in shape:
                n *= s
            assert at + n <= ARENA, (at, n)
            v = arena[:, at:at + n]
            if len(shape) == 1:
                return v
            names = "abcd"[:len(shape)]
            return v.rearrange(f"p ({' '.join(names)}) -> p {' '.join(names)}",
                               **{k: s for k, s in zip(names, shape)})

        def slot(s, *shape):
            n = 1
            for k in shape:
                n *= k
            names = "abcd"[:len(shape)]
            return ring[:, s, 0:n].rearrange(f"p ({' '.join(names)}) -> p {' '.join(names)}",
                                             **{k: v for k, v in zip(names, shape)})

        def bank(i, *shape):
            n = 1
            for k in shape:
                n *= k
            names = "abcd"[:len(shape)]
            return ps[i][:, 0:n].rearrange(f"p ({' '.join(names)}) -> p {' '.join(names)}",
                                           **{k: v for k, v in zip(names, shape)})

        lam_re, lam_im = cols[:, 0, 96:112], cols[:, 0, 112:128]
        C_PSCALE, C_S5D, C_M2G, C_CONVB, C_C = 64, 68, 72, 88, 120

        def norm_col(layer, i):
            at = (layer * 4 + i) * KC
            return cols[:, 1, at:at + KC]

        tables = ring[:, 4:6, :].rearrange("p k (q t) -> p k q t", q=NQ)
        bt = slot(6, NQ, 2, P)
        rows = slot(3, 3, P)
        t_row = ring[:, 3, 512:512 + TOK]
        inv_cnt = ring[:, 3, 1024:2048].rearrange("p (g t) -> p g t", g=4)
        hT = area(0, KC, TOK)
        yT = area(0, KC, TOK)
        ct = area(2048, NQ, 3, P)
        band = area(8192, 4, NB, TOK)
        u_tok = area(10240, NB, HALF)
        uT = area(11264, 4, TOK)
        ys = area(12288, 4, TOK)
        b_raw, bb = area(10240, 2, NQ, 16), area(10752, 2, NQ, 16)
        c_raw = area(12288, 2, 4, P)
        grow = area(13312, D)
        modpart = area(13312, HALF)
        temps = area(14336, 2, 2, 2, TOK)
        zz = area(16384, 2, 2, TOK)
        qq = area(17408, 2, 2, 2, TOK)
        xn = area(14336, NB, D)
        tmp = area(14336, NB, D)
        bx = area(14336, 2, NQ, P)
        pw = area(18432, 4, P)
        pool_in = area(18944, 2, TOK)
        STEP, LRSTEP, MAG, LR, TAU, PA, FR, FI, PB, PC, INV = range(11)
        prm = hd[:, 0:3].rearrange("p a b c -> p (a b c)").rearrange("p (r q) -> p r q", q=NQ)
        log_step = prm[:, FR:FI + 1].rearrange("p a q -> p (a q)")
        act_f = area(2048, 2, 4, TOK)
        silu_f = area(4096, 2, TOK)
        xs = area(2048, NB, INNER)
        zs = area(6144, NB, INNER)
        bc = slot(6, 2, NG, TOK)
        btok = area(10240, NG, P)
        conv = area(12288, 2, TOK)
        xsT = area(12800, 2, TOK)
        dmin = area(13312, 2, HALF)
        mix = area(14336, 2, HALF)
        cbm = area(15360, 2, P)
        xdt = area(15616, 2, TOK)
        xw = area(12288, 2, TOK)
        xd = area(12800, 2, TOK)
        yo = area(16128, 2, TOK)
        st = area(16640, NG, TOK)
        junk_y = area(12288, INNER)
        yT1 = area(2048, 16, TOK)
        grow1 = area(11264, D)
        h_tok = area(0, NB, D)
        hgT = area(2048, NE, KC, P)
        HG_AT, GT_AT = 2048, 10240
        gT = area(GT_AT, NE, TOK)
        acc = area(12288, NB, D)
        hcur = area(14336, KC * P)
        hcur3 = area(14336, KC, P)
        gcur = dtw.rearrange("p a b -> p (a b)")
        sg = area(15360, 2, HALF)
        actT = area(16384, 2, 2, 4, P)
        y_sb = area(18432, D)
        hot = area(15360, NB, 2, P)
        hotg = area(15872, NB, 2, P)
        xn2 = area(2048, NB, D)
        gsrow, shrow = area(4096, D), area(5120, D)
        hT2 = area(16384, KC, TOK)
        tmp2 = area(14336, NB, D)
        DT, DA, ECS, TOEND, TMP0, TMP1 = range(6)
        LOGIT, EXPS, SEL, GATE, POS, RANK = range(6)

        names = """small_in x_in s5_in pw_in l1_in consts t_iota rows_turned cols_ready cT_zero c_ready
            ada_copied ada_turned mod_ready inv_ready band_ready
            step_exp step_ready mag_ready tab_ready tab_sin bx_ready b_turned bt_ready c_turned ct_zero ct_ready
            xn_ready turned hT_low hT_high gs_ready u_ready pool_mm pool_in_ready pool_out_mm pool_out
            bu_mm bu_used z_ready q_ready y_mm yskip ys_ready glu_mm glu_sig yT_ready gg_ready grow_mm grow_ready
            sq_done rg_ready root_in root_done x_ready dve_step act_step
            f_mm f_silu f_act
            dt_mm dt_pre dt_exp dt_ln a_exp da_ready cs_mm cs_exp
            xbc_mm conv_done silu_done xs_turned xs_ready b_turned1 btok_ready z_mm z_silu
            dec_mm dec_min dec_exp cb_mm cbm_ready m_ready xw_ready xdt_ready y1_mm st_mm st_ready y_ready
            y_turned yT1_a yT1_b row_mm row_ready htok_ready h2_turned h2_low h2_high logit_mm rt_pre rt_exp
            mask_ready pos_mm pos_ready cnt_ready acc_zero hot_ready gather_mm hg_ready gT_mm gT_ready
            hcur_ready gcur_ready e_silu e_act e_turned actT_ready y_low y_high scat_mm acc_done
            last_sum last_root last_mm final stored tile_used""".split()
        s = {n: sem(n) for n in names}
        ring_full = [sem(f"ring_full{i}") for i in range(RING)]
        block = ctx.enter_context(nc.Block())

        class Counted:

            def __init__(self, eng):
                self.eng, self.n = eng, {}

            def inc(self, ins, name):
                ins.then_inc(s[name], 1)
                self.n[name] = self.n.get(name, 0) + 1

            def then(self, ins, name):
                self.inc(ins, name)
                self.eng.wait_ge(s[name], self.n[name])

        def w_cols(w, at, n):
            return w.rearrange("(k p) n -> p k n", p=P)[:, :, at:at + n]

        def w_rows(w, at, n):
            return w[at:at + n * P, :].rearrange("(k p) n -> p k n", p=P)

        PRIMED = {"pe": ("gather_mm", "gT_mm", "e_turned", "scat_mm"), "act": ("hg_ready", "e_silu", "actT_ready", "y_low"),
                  "dve": ("gT_ready", "hot_ready", "e_act", "y_high", "acc_done", "pos_ready"),
                  "pool": ("hcur_ready", "gcur_ready")}

        def past(eng, name, n):
            eng.wait_ge(s[name], n + 1)

        def items_loop(eng, name, prep, item, by_blocks):
            eng.wait_ge(s["cnt_ready"], 1)
            for primed in PRIMED[name]:
                eng.sem_inc(s[primed], 1)
            items = ctx.enter_context(eng.register(f"{name}_items"))
            eng.reg_mov(items, 0)
            with eng.Fori(0, 2) as p:
                run = eng.value_load(cnt[0:1, bass.ds(p * 16, 1)])
                with eng.If(run > 0):
                    if prep is not None:
                        prep(p)
                    with eng.Fori(0, NE) as e:
                        n = eng.value_load(cnt[0:1, bass.ds(p * NE + e, 1)])
                        with eng.If(n > 0):
                            k = eng.snap(items)
                            if by_blocks:
                                with eng.If(n > 64):
                                    item(p, e, k, 2)
                                with eng.Else():
                                    item(p, e, k, 1)
                            else:
                                item(p, e, k, 2)
                            eng.reg_add(items, items, 1)
            return items

        @block.sync
        def _(sp):
            def part(w, n, total):
                return w_cols(w, n * HALF, min(HALF, total - n * HALF)), KC, min(HALF, total - n * HALF)

            def down(n):
                k = min(4, (FFN - n * HALF) // P)
                return w_rows(a["ffn_w_down"][0], n * HALF, k), k, D
            sources = {
                "ada0": lambda n: part(a["ada_w"][0], n, 6 * D), "ada1": lambda n: part(a["ada_w"][1], n, 6 * D),
                "mixin": lambda n: part(a["mix_w_in"][0], n, D), "mixout": lambda n: part(a["mix_w_out"][0], n, D),
                "glu": lambda n: (w_cols(a["s5_w_glu"][0], 0, HALF), 4, HALF),
                "gate": lambda n: part(a["ffn_w_gate"][0], n, FFN), "up": lambda n: part(a["ffn_w_up"][0], n, FFN),
                "down": down,
                "xbc": lambda n: (w_cols(a["m2_w_in"][0], INNER + n * HALF, HALF), KC, HALF),
                "z": lambda n: (w_cols(a["m2_w_in"][0], n * HALF, HALF), KC, HALF),
                "m2out": lambda n: (w_rows(a["m2_w_out"][0], n * HALF, 4), 4, D),
            }
            for i, (kind, n, sl) in enumerate(TILES):
                src, k, w = sources[kind](n)
                if LAST_USER[i] is not None:
                    sp.wait_ge(s["tile_used"], LAST_USER[i] + 1)
                elif sl == 3:
                    sp.wait_ge(s["rows_turned"], 1)
                    sp.wait_ge(s["tab_ready"], 1)
                    sp.wait_ge(s["band_ready"], 4)
                elif sl in (4, 5):
                    sp.wait_ge(s["q_ready"], 2 * NQ)
                    sp.wait_ge(s["z_ready"], 2 * NQ)
                elif sl == 6:
                    sp.wait_ge(s["bu_mm"], NQ)
                sp.dma_start(slot(sl, k, w), src).then_inc(ring_full[sl], 16)

            wg = a["moe_w_gate"][0].rearrange("e (k p) n -> e p k n", p=P)
            wu = a["moe_w_up"][0].rearrange("e (k p) n -> e p k n", p=P)
            wd = a["moe_w_down"][0].rearrange("e (k p) n -> e p k n", p=P)

            def load_expert(e, k):
                for what, t, m in ORDER:
                    for h in range(m):
                        j = FIRST[what, t] + h
                        sp.wait_ge(s["tile_used"], k * ITEM + (MOE0 + j - RING + 1))
                        if what == "d":
                            dst = slot(j % RING, 4, D)
                            src = wd[bass.ds(e, 1), :, t * 8 + 4 * h:t * 8 + 4 * h + 4, :]
                        else:
                            dst = slot(j % RING, KC, HALF)
                            src = (wg if what == "g" else wu)[bass.ds(e, 1), :, :, (2 * t + h) * HALF:(2 * t + h + 1) * HALF]
                        sp.dma_start(dst, src.rearrange("e p k n -> p (e k) n")).then_inc(ring_full[j % RING], 16)

            with sp.Fori(0, NE) as e:
                load_expert(e, e)
            sp.wait_ge(s["cnt_ready"], 1)
            with sp.register("sp_items") as items:
                sp.reg_mov(items, NE)
                over = sp.value_load(cnt[0:1, 16:17])
                with sp.If(over > 0):
                    with sp.Fori(0, NE) as e:
                        n = sp.value_load(cnt[0:1, bass.ds(e + NE, 1)])
                        with sp.If(n > 0):
                            load_expert(e, sp.snap(items))
                            sp.reg_add(items, items, 1)
            for b in range(NB):
                sp.wait_ge(s["final"], b + 1)
                sp.dma_start(out[0, b * P:(b + 1) * P, :], x[:, b, :]).then_inc(s["stored"], 16)
            sp.wait_ge(s["stored"], 16 * NB)

        @block.gpsimd
        def _(pool):
            c = Counted(pool)
            g = nc.gpsimd
            for dst, v, op, pattern, cm in (
                    (ident[:, :], 0.0, ALU.not_equal, [[-1, P]], 1), (tri[:, :], 1.0, ALU.is_ge, [[1, P]], -1),
                    (ntri[:, :], -1.0, ALU.is_ge, [[1, P]], -1), (after[:, :], 1.0, ALU.is_gt, [[-1, P]], 1),
                    (earlier[:, :, :], 1.0, ALU.is_gt, [[1, NE], [-1, NE]], 0)):
                c.then(g.memset(dst, v), "consts")
                c.inc(g.affine_select(out=dst, in_=dst, compare_op=op, fill=1.0 if op == ALU.not_equal else 0.0,
                                      base=0, pattern=pattern, channel_multiplier=cm), "consts")
                if v == 0.0:
                    c.inc(g.iota(t_row, [[1, TOK]], base=0, channel_multiplier=0,
                                 allow_small_or_imprecise_dtypes=True), "t_iota")
            c.inc(g.memset(ones[:, :], 1.0), "consts")
            c.inc(g.iota(slot_iota[:, :], [[1, P]], base=0, channel_multiplier=0,
                         allow_small_or_imprecise_dtypes=True), "consts")
            for i, win in enumerate(POOL_WINDOWS):
                b = band[:, i]
                c.then(g.memset(b, 1.0), "consts")
                c.then(g.affine_select(out=b, in_=b, compare_op=ALU.is_ge, fill=0.0, base=0,
                                       pattern=[[-P, NB], [1, TOK]], channel_multiplier=-1), "consts")
                c.then(g.affine_select(out=b, in_=b, compare_op=ALU.is_ge, fill=0.0, base=win - 1,
                                       pattern=[[P, NB], [-1, TOK]], channel_multiplier=1), "consts")
                pool.wait_ge(s["inv_ready"], 1)
                c.then(g.tensor_tensor(b, b, inv_cnt[:, i:i + 1].broadcast_to([P, NB, TOK]), ALU.mult), "band_ready")
            for b in range(NB):
                v = band[:, :, b, b * P:(b + 1) * P]
                c.then(g.tensor_tensor(v, v, ident[:, :].unsqueeze(1).broadcast_to([P, 4, P]), ALU.subtract), "band_ready")
            pool.wait_ge(s["tab_sin"], 2)
            pool.wait_ge(s["pool_out"], 4)
            for q in range(NQ):
                pool.wait_ge(s["z_ready"], 2 * (q + 1))
                if q >= 2:
                    pool.wait_ge(s["y_mm"], q - 1)
                for k in range(2):
                    c.inc(g.tensor_tensor(qq[:, q % 2, k], zz[:, q % 2],
                                          tables[:, 1 - k, q:q + 1, :].broadcast_to([P, 2, TOK]), ALU.mult), "q_ready")
            pool.wait_ge(s["xs_ready"], 8)
            pool.wait_ge(s["da_ready"], 1)
            pool.wait_ge(s["l1_in"], 96)
            for n in range(NB * NG):
                blk, grp = n // NG, n % NG
                if n >= 2:
                    pool.wait_ge(s["y_ready"], n - 1)
                src = xs[:, blk, TOK * grp:TOK * grp + TOK].rearrange("p (j c) -> p j c", j=4)
                for dst, v in ((xdt, hd[:, DT, blk, 4 * grp:4 * grp + 4]),
                               (xd, bro[:, 2 * HEADS + 4 * grp:2 * HEADS + 4 * grp + 4])):
                    c.inc(g.tensor_tensor(dst[:, n % 2].rearrange("p (j c) -> p j c", j=4), src,
                                          v.unsqueeze(2).broadcast_to([P, 4, 64]), ALU.mult), "xdt_ready")

            def item(p, e, k, nb):
                past(pool, "hg_ready", p * 16 + 16)
                pool.wait_ge(s["tile_used"], k * ITEM + MOE0)
                g.tensor_copy(hcur, arena[:, bass.ds(e * (KC * P) + HG_AT, KC * P)]).then_inc(s["hcur_ready"], 1)
                past(pool, "gT_ready", p * 4 + 4)
                past(pool, "scat_mm", k * 4)
                g.tensor_copy(gcur, arena[:, bass.ds(e * TOK + GT_AT, TOK)]).then_inc(s["gcur_ready"], 1)
            items_loop(pool, "pool", None, item, False)

        @block.scalar
        def _(act):
            c = Counted(act)
            f = nc.scalar.activation

            def load(dst, src, name):
                act.dma_start(dst, src).then_inc(s[name], 16)

            def by_p(v):
                return v.rearrange("(r p) -> r p", p=P)
            load(rows[120:128, 1, :], by_p(a["c"][0]), "small_in")
            load(rows[0:96, 0, :], a["ada_b"].rearrange("l (r p) -> (l r) p", p=P), "small_in")
            load(rows[0:64, 1, :], a["norm_g"].rearrange("l i (r p) -> (l i r) p", p=P), "small_in")
            load(rows[96:112, 0, :], a["s5_lam_re"][0].rearrange("(r g) n -> r (g n)", g=2), "small_in")
            load(rows[112:128, 0, :], a["s5_lam_im"][0].rearrange("(r g) n -> r (g n)", g=2), "small_in")
            load(rows[64:68, 1, :], by_p(a["pool_scale"][0]), "small_in")
            load(rows[68:72, 1, :], by_p(a["s5_d"][0]), "small_in")
            load(rows[72:88, 1, :], by_p(a["m2_norm_g"][0]), "small_in")
            load(rows[88:120, 1, :], by_p(a["m2_conv_b"][0]), "small_in")
            load(rows[:, 2, :], a["m2_conv_w"][0].rearrange("k (r p) -> (k r) p", p=P), "small_in")
            load(x[:, :, :], a["x"][0].rearrange("(b p) d -> p b d", p=P), "x_in")
            load(log_step, a["s5_log_step"].broadcast_to([P, 2 * NQ]), "s5_in")
            for i, n in enumerate(("s5_b_re", "s5_b_im")):
                load(b_raw[:, i], a[n][0].rearrange("(q g) n h -> (g n) q h", g=2), "s5_in")
            for i, n in enumerate(("s5_c_re", "s5_c_im")):
                for h in range(2):
                    load(c_raw[:, i, :, 64 * h:64 * h + 64], a[n][0].rearrange("(m g) h n -> (g h) m n", m=4), "s5_in")
            load(pw, a["pool_w"][0].rearrange("g p n -> p g n"), "pw_in")
            load(dtw[:, :, :], w_cols(a["m2_w_in"][0], INNER + 4096, HEADS), "l1_in")
            load(rw[:, :, :], w_cols(a["moe_w_router"][0], 0, NE), "l1_in")
            at = 0
            for n, w in (("m2_dt_bias", HEADS), ("m2_a_log", HEADS), ("m2_d", HEADS), ("moe_b_router", NE)):
                load(bro[:, at:at + w], a[n].broadcast_to([P, w]), "l1_in")
                at += w

            def ada(i):
                act.wait_ge(s["tile_used"], ADA[i] + 1)
                if i:
                    act.wait_ge(s["ada_turned"], i)
                c.inc(f(modpart, ps[6][:, :], ACT.Copy), "ada_copied")

            def squares(dst):
                for b in range(NB):
                    c.inc(f(dst[:, b], x[:, b], ACT.Square, accum_out=stat[:, b:b + 1]), "sq_done")
                act.wait_ge(s["sq_done"], c.n["sq_done"])
                c.inc(f(stat[:, 2:4], stat[:, 0:2], ACT.Sqrt, bias=eps[:, 0:1], scale=1.0 / D), "root_done")

            def y_squares(n, base=0, prescale=None):
                for i in range(4):
                    scale = 1.0 if prescale is None else prescale[:, i // 2:i // 2 + 1]
                    c.inc(f(tmp[:, i // 2, HALF * (i % 2):HALF * (i % 2) + HALF], ps[base + i][:, :], ACT.Square,
                            scale=scale, accum_out=stat[:, 4 + i:5 + i]), "sq_done")
                act.wait_ge(s["root_in"], n)
                c.inc(f(stat[:, 10:12], stat[:, 8:10], ACT.Sqrt, bias=eps[:, 0:1], scale=1.0 / D), "root_done")

            def hT_high(n, n_mod, shift):
                act.wait_ge(s["turned"], n)
                act.wait_ge(s["gs_ready"], n)
                act.wait_ge(s["mod_ready"], n_mod)
                for kc in range(KC // 2, KC):
                    c.inc(f(hT[:, kc], bank(kc // 2, 2, TOK)[:, kc % 2], ACT.Identity, bias=shift[:, kc:kc + 1],
                            scale=gs[:, kc:kc + 1]), "hT_high")

            def grow_rows(n, dst, base=4):
                act.wait_ge(s["grow_mm"], n)
                for h in range(2):
                    c.inc(f(dst[:, HALF * h:HALF * h + HALF], ps[base + h][:, :], ACT.Copy), "grow_ready")

            act.wait_ge(s["cT_zero"], 2)
            act.wait_ge(s["cols_ready"], 1)
            c.inc(f(cT[:, :, 0], cols[:, 1, C_C:C_C + KC], ACT.Silu), "c_ready")
            act.wait_ge(s["x_in"], 16)
            squares(xn)
            act.wait_ge(s["s5_in"], 112)
            for h in range(2):
                rows_h = slice(64 * h, 64 * h + 64)
                c.inc(f(prm[rows_h, STEP], log_step[rows_h, h:2 * NQ:2], ACT.Exp), "step_exp")
            act.wait_ge(s["step_ready"], 1)
            c.inc(f(prm[:, MAG], prm[:, LRSTEP], ACT.Exp), "mag_ready")
            ada(0)
            ada(1)
            act.wait_ge(s["c_turned"], 1)
            act.wait_ge(s["ct_zero"], 1)
            for h in range(2):
                for j in range(4):
                    at = 32 * j + 16 * h
                    for k, i, sign in ((0, 0, 1.0), (1, 1, 1.0), (2, 1, -1.0)):
                        src = bank(2 + i, 4, P)[64 * h:64 * h + 64, :, at:at + 16]
                        dst = ct[64 * h:64 * h + 64, j:NQ:4, k, at:at + 16]
                        c.inc(f(dst, src, ACT.Copy, scale=sign), "ct_ready")
            ada(2)
            act.wait_ge(s["tab_ready"], 2)
            for k in range(2):
                c.inc(f(tables[:, k], tables[:, k], ACT.Sin, scale=TWO_PI), "tab_sin")
            ada(3)
            hT_high(1, 4, mod[:, 0, 0])
            for i in range(8):
                act.wait_ge(s["b_turned"], i + 1)
                c.inc(f(bt[:, 2 * i:2 * i + 2], bank(4 + i % 2, 2, 2, P), ACT.Copy), "bt_ready")
            act.wait_ge(s["tile_used"], AT["mixin", 0] + 1)
            for b in range(NB):
                c.inc(f(u_tok[:, b], ps[4 + b][:, :], ACT.Copy), "u_ready")
            act.wait_ge(s["tile_used"], AT["mixin", 1] + 1)
            for h in range(2):
                c.inc(f(uT[:, 2 * h:2 * h + 2], bank(h, 2, TOK), ACT.Copy), "u_ready")
            for i in range(4):
                act.wait_ge(s["pool_mm"], i + 1)
                c.inc(f(pool_in[:, i % 2], ps[i % 2][:, 0:TOK], ACT.Copy), "pool_in_ready")
                act.wait_ge(s["pool_out_mm"], i + 1)
                c.inc(f(yT[:, i], ps[i % 2][:, TOK:HALF], ACT.Copy,
                        scale=cols[:, 1, C_PSCALE + i:C_PSCALE + i + 1]), "pool_out")

            def gelu(m):
                act.wait_ge(s["yskip"], m + 1)
                c.inc(f(ys[:, m], ys[:, m], ACT.Gelu_apprx_tanh), "ys_ready")
            for q in range(NQ):
                if q % 2:
                    ada(4 + q // 2)
                if q in (6, 10, 14):
                    gelu((q - 6) // 4)
            gelu(3)
            for m in range(4):
                act.wait_ge(s["glu_mm"], m + 1)
                c.inc(f(uT[:, m], ps[m][:, 0:TOK], ACT.Sigmoid), "glu_sig")
            act.wait_ge(s["ada_turned"], NADA)
            grow_rows(1, grow)
            act.wait_ge(s["tile_used"], AT["mixout", 1] + 1)
            act.wait_ge(s["q_ready"], 2 * NQ)
            y_squares(1)
            act.wait_ge(s["x_ready"], 2)
            squares(xn)
            hT_high(2, NADA, mod[:, 0, 3])

            for t in range(6):
                for j in range(2 if t == 5 else 4):
                    n = 4 * t + j
                    act.wait_ge(s["f_mm"], 2 * n + 1)
                    if n >= 2:
                        act.wait_ge(s["f_act"], n - 1)
                    c.inc(f(silu_f[:, n % 2], ps[4][:, 0:TOK], ACT.Silu), "f_silu")
                ada(NADA + 2 * t)
                ada(NADA + 2 * t + 1)
            act.wait_ge(s["ada_turned"], 2 * NADA)
            grow_rows(2, grow)
            act.wait_ge(s["tile_used"], AT["down", 5] + 1)
            y_squares(2)

            act.wait_ge(s["x_ready"], 4)
            squares(xn)
            hT_high(3, 2 * NADA, mod[:, 1, 0])
            act.wait_ge(s["l1_in"], 96)
            c.inc(f(hd[:, TMP1, 0], bro[:, HEADS:2 * HEADS], ACT.Exp), "a_exp")
            act.wait_ge(s["dt_pre"], 1)
            c.then(f(hd[:, TMP0], hd[:, TMP0], ACT.Exp), "dt_exp")
            c.inc(f(hd[:, TMP0], hd[:, TMP0], ACT.Ln, bias=1.0), "dt_ln")

            def xs_copy(m):
                act.wait_ge(s["xs_turned"], 2 * m + 2)
                c.inc(f(xs[:, :, 2 * P * m:2 * P * (m + 1)], bank(4 + m % 2, NB, 2 * P), ACT.Copy), "xs_ready")
            for n in range(32):
                act.wait_ge(s["conv_done"], n + 1)
                if n < 16:
                    if n >= 2:
                        act.wait_ge(s["xs_turned"], n - 1)
                    dst = xsT[:, n % 2]
                else:
                    if n == 16:
                        act.wait_ge(s["tile_used"], LAST_SLOT6 + 1)
                    dst = bc[:, n // 8 - 2, n % 8]
                c.inc(f(dst, conv[:, n % 2], ACT.Silu), "silu_done")
                if n == 4:
                    act.wait_ge(s["cs_mm"], 1)
                    c.inc(f(hd[:, ECS:TOEND + 1], ps[6][:, P:2 * P].rearrange("p (k b h) -> p k b h", k=2, b=NB), ACT.Exp), "cs_exp")
                if n % 2 and 3 <= n <= 17:
                    xs_copy((n - 3) // 2)
                if n in (21, 25):
                    h = (n - 21) // 4
                    act.wait_ge(s["b_turned1"], 4 * h + 4)
                    c.inc(f(btok[:, 4 * h:4 * h + 4], bank(4 + h, 4, P), ACT.Copy), "btok_ready")
            for n in range(NB * NG):
                act.wait_ge(s["dec_min"], n + 1)
                c.inc(f(dmin[:, n % 2], dmin[:, n % 2], ACT.Exp), "dec_exp")
                if n % 2:
                    zi = n // 2
                    act.wait_ge(s["z_mm"], zi + 1)
                    b, sl = zi // 4, zi % 4
                    c.inc(f(zs[:, b, HALF * sl:HALF * sl + HALF], ps[6 + zi % 2][:, :], ACT.Silu), "z_silu")
                if 1 <= n <= NG:
                    act.wait_ge(s["st_mm"], n)
                    c.inc(f(st[:, n - 1], ps[4][:, TOK * ((n - 1) % 2):TOK * ((n - 1) % 2) + TOK], ACT.Copy), "st_ready")
            act.wait_ge(s["y_ready"], NB * NG)
            for b in range(NB):
                c.then(f(junk_y, zs[:, b], ACT.Square, accum_out=stat[:, 12 + b:13 + b]), "sq_done")
            c.inc(f(stat[:, 14:16], stat[:, 12:14], ACT.Sqrt, bias=eps[:, 0:1], scale=1.0 / INNER), "root_done")
            grow_rows(3, grow1, 0)
            for m in range(1, 8, 2):
                act.wait_ge(s["y_turned"], m + 1)
                for n in (2 * m, 2 * m + 1):
                    c.inc(f(yT1[:, n], bank(m % 4, 2, TOK)[:, n % 2], ACT.Copy,
                            scale=cols[:, 1, C_M2G + n:C_M2G + n + 1]), "yT1_b")
            act.wait_ge(s["tile_used"], MOE0)
            act.wait_ge(s["rg_ready"], 1)
            y_squares(3, 4, rst[:, 4:6])

            act.wait_ge(s["x_ready"], 6)
            squares(xn2)
            act.wait_ge(s["row_mm"], 1)
            for h in range(4):
                dst = (gsrow, shrow)[h // 2]
                c.inc(f(dst[:, HALF * (h % 2):HALF * (h % 2) + HALF], ps[h][:, :], ACT.Copy), "row_ready")
            act.wait_ge(s["h2_turned"], 1)
            for i in (2, 3):
                c.inc(f(hT2[:, 2 * i:2 * i + 2], bank(4 + i, 2, TOK), ACT.Copy), "h2_high")
            act.wait_ge(s["rt_pre"], 1)
            c.inc(f(rt[:, EXPS], rt[:, EXPS], ACT.Exp), "rt_exp")

            def prep(p):
                past(act, "hcur_ready", p * NE)
                for ep in range(4):
                    past(act, "gather_mm", p * 4 + ep + 1)
                    for i in range(4):
                        dst = hgT[:, 2 * ep:2 * ep + 2, 2 * i:2 * i + 2, :].rearrange("p e c n -> p c e n")
                        f(dst, bank(i, 2, 2, P), ACT.Copy).then_inc(s["hg_ready"], 1)

            def item(p, e, k, nb):
                def to_hidden(t):
                    past(act, "e_turned", k * 4 + t + 1)
                    for b in range(nb):
                        w = WIDTHS[t] // P
                        ins = f(actT[:, t % 2, b, 0:w], bank(6 + b, w, P), ACT.Copy)
                    ins.then_inc(s["actT_ready"], 1)
                for t in range(4):
                    act.wait_ge(s["tile_used"], k * ITEM + (MOE0 + DONE["g", t]))
                    past(act, "e_turned", k * 4 + t)
                    for b in range(nb):
                        ins = f(sg[:, b, 0:WIDTHS[t]], ps[b][:, 0:WIDTHS[t]], ACT.Silu)
                    ins.then_inc(s["e_silu"], 1)
                    if t:
                        to_hidden(t - 1)
                to_hidden(3)
                act.wait_ge(s["tile_used"], k * ITEM + (MOE0 + ITEM))
                for b in range(nb):
                    ins = f(y_sb[64 * b:64 * b + 64, 0:HALF], ps[4 + b][0:64, :], ACT.Copy)
                ins.then_inc(s["y_low"], 1)
            items_loop(act, "act", prep, item, True)
            act.wait_ge(s["last_sum"], 1)
            f(stat[:, 10:12], stat[:, 8:10], ACT.Sqrt, bias=eps[:, 0:1], scale=1.0 / D).then_inc(s["last_root"], 1)

        @block.vector
        def _(dve):
            c = Counted(dve)
            v = nc.vector
            tt, ts, stt = v.tensor_tensor, v.tensor_scalar, v.scalar_tensor_tensor
            step = "dve_step"

            def root(n):
                dve.wait_ge(s["root_done"], n)

            def mods(i):
                dve.wait_ge(s["ada_turned"], i + 1)
                m = modraw[:, i % 2]
                c.then(v.tensor_reduce(m, bank(7, 4, 4, 32)[:, :, :, 0], AX.X, ALU.add), step)
                layer, n = i // NADA, i % NADA
                at = layer * 48 + 4 * n
                c.inc(tt(mod_flat[:, at:at + 4], m, cols[:, 0, at:at + 4], ALU.add), "mod_ready")

            def norm_x(dst, n_root):
                root(n_root)
                c.then(v.reciprocal(rst[:, 0:2], stat[:, 2:4]), step)
                for b in range(NB):
                    c.inc(ts(dst[:, b], x[:, b], rst[:, b:b + 1], None, ALU.mult), "xn_ready")

            def scale_cols(n, n_mod, scale, g):
                dve.wait_ge(s["mod_ready"], n_mod)
                if n > 1:
                    dve.wait_ge(s["hT_high"], 4 * (n - 1))
                c.then(stt(gs[:, :], scale, 1.0, g, ALU.add, ALU.mult), "gs_ready")

            def hT_low(n, shift):
                dve.wait_ge(s["turned"], n)
                for kc in range(KC // 2):
                    c.inc(ts(hT[:, kc], bank(kc // 2, 2, TOK)[:, kc % 2], gs[:, kc:kc + 1], shift[:, kc:kc + 1],
                             ALU.mult, ALU.add), "hT_low")

            def gate_cols(n, gate, g):
                dve.wait_ge(s["mod_ready"], c.n["mod_ready"])
                if n > 1:
                    dve.wait_ge(s["grow_mm"], n - 1)
                c.inc(tt(gg[:, :], gate, g, ALU.mult), "gg_ready")

            def residual(n, n_sq, n_root, rows_, base=0, prescaled=False):
                dve.wait_ge(s["sq_done"], n_sq)
                c.inc(tt(stat[:, 8:10], stat[:, 4:8:2], stat[:, 5:8:2], ALU.add), "root_in")
                root(n_root)
                c.then(v.reciprocal(rst[:, 2:4], stat[:, 10:12]), step)
                if prescaled:
                    c.then(tt(rst[:, 2:4], rst[:, 2:4], rst[:, 4:6], ALU.mult), step)
                dve.wait_ge(s["grow_ready"], 2 * n)
                for b in range(NB):
                    for h in range(2):
                        c.inc(stt(tmp[:, b, HALF * h:HALF * h + HALF], ps[base + 2 * b + h][:, :], rst[:, 2 + b:3 + b],
                                  rows_[:, HALF * h:HALF * h + HALF], ALU.mult, ALU.mult), step)
                    dve.wait_ge(s[step], c.n[step])
                    c.inc(tt(x[:, b], x[:, b], tmp[:, b], ALU.add), "x_ready")
                dve.wait_ge(s["x_ready"], 2 * n)

            c.inc(v.memset(cT[:, :, :], 0.0), "cT_zero")
            c.inc(v.memset(eps[:, :], EPS), "cT_zero")
            dve.wait_ge(s["s5_in"], 112)
            dve.wait_ge(s["rows_turned"], 1)
            c.then(v.tensor_copy(cols[:, :, :], bank(0, 3, P)), "cols_ready")
            c.then(ts(prm[:, LR], lam_re, -1e-4, None, ALU.min), step)
            dve.wait_ge(s["step_exp"], 2)
            c.inc(tt(prm[:, LRSTEP], prm[:, LR], prm[:, STEP], ALU.mult), "step_ready")
            c.then(tt(prm[:, TAU], lam_im, prm[:, STEP], ALU.mult), step)
            c.then(ts(prm[:, TAU], prm[:, TAU], INV_TWO_PI, None, ALU.mult), step)
            c.then(ts(prm[:, PA], prm[:, TAU], ROUND, -ROUND, ALU.add, ALU.add), step)
            c.then(tt(prm[:, TAU], prm[:, TAU], prm[:, PA], ALU.subtract), step)
            dve.wait_ge(s["t_iota"], 1)
            for i, win in enumerate(POOL_WINDOWS):
                c.inc(ts(inv_cnt[:, i], t_row, 1.0, float(win), ALU.add, ALU.min), step)
            dve.wait_ge(s[step], c.n[step])
            c.inc(v.reciprocal(inv_cnt, inv_cnt), "inv_ready")
            tS, tC = tables[:, 0], tables[:, 1]
            c.then(tt(tS, t_row.unsqueeze(1).broadcast_to([P, NQ, TOK]),
                      prm[:, TAU].unsqueeze(2).broadcast_to([P, NQ, TOK]), ALU.mult), "tab_ready")
            norm_x(xn, 1)
            mods(0)
            c.then(ts(tC, tS, ROUND, -ROUND, ALU.add, ALU.add), step)
            c.then(tt(tS, tS, tC, ALU.subtract), step)
            mods(1)
            c.inc(v.memset(ct, 0.0), "ct_zero")
            c.then(ts(tC, tS, 0.25, None, ALU.is_gt), step)
            c.inc(stt(tC, tS, 0.25, tC, ALU.add, ALU.subtract), "tab_ready")
            mods(2)
            dve.wait_ge(s["turned"], 1)
            c.then(v.memset(bx, 0.0), step)
            mods(3)
            scale_cols(1, 4, mod[:, 0, 1], norm_col(0, 0))
            hT_low(1, mod[:, 0, 0])
            dve.wait_ge(s["tab_sin"], 2)
            dve.wait_ge(s["mag_ready"], 1)
            c.then(tt(prm[:, PA], prm[:, MAG], tC[:, :, 1], ALU.mult), step)
            c.then(tt(prm[:, PB], prm[:, MAG], tS[:, :, 1], ALU.mult), step)
            c.then(ts(prm[:, PA], prm[:, PA], -1.0, None, ALU.add), step)
            c.then(tt(prm[:, PC], prm[:, LR], prm[:, LR], ALU.mult), step)
            c.then(tt(prm[:, INV], lam_im, lam_im, ALU.mult), step)
            c.then(tt(prm[:, INV], prm[:, INV], prm[:, PC], ALU.add), step)
            c.then(v.reciprocal(prm[:, INV], prm[:, INV]), step)
            for dst, p1, p2, op in ((FR, PA, PB, ALU.add), (FI, PB, PA, ALU.subtract)):
                c.then(tt(prm[:, dst], prm[:, p1], prm[:, LR], ALU.mult), step)
                c.then(tt(prm[:, PC], prm[:, p2], lam_im, ALU.mult), step)
                c.then(tt(prm[:, dst], prm[:, dst], prm[:, PC], op), step)
                c.then(tt(prm[:, dst], prm[:, dst], prm[:, INV], ALU.mult), step)
            fr = prm[:, FR].unsqueeze(2).broadcast_to([P, NQ, 16])
            fi = prm[:, FI].unsqueeze(2).broadcast_to([P, NQ, 16])
            for dst, other, op in ((0, 1, ALU.subtract), (1, 0, ALU.add)):
                c.then(tt(bb[:, dst], b_raw[:, dst], fr, ALU.mult), step)
                w = s5_tmp[:, :, :]
                c.then(tt(w, b_raw[:, other], fi, ALU.mult), step)
                c.then(tt(bb[:, dst], bb[:, dst], w, op), step)
            for h in range(2):
                for j in range(4):
                    at = 32 * j + 16 * h
                    c.inc(v.tensor_copy(bx[64 * h:64 * h + 64, :, j:NQ:4, at:at + 16],
                                        bb[64 * h:64 * h + 64, :, j:NQ:4, :]), "bx_ready")

            def skip(m):
                dve.wait_ge(s["y_mm"], 4 * m + 4)
                c.inc(stt(ys[:, m], uT[:, m], cols[:, 1, C_S5D + m:C_S5D + m + 1], ps[4 + m % 2][:, 0:TOK],
                          ALU.mult, ALU.add), "yskip")
            dve.wait_ge(s["u_ready"], 4)
            dve.wait_ge(s["b_turned"], 8)
            for q in range(NQ):
                t = temps[:, q % 2]
                dve.wait_ge(s["bu_mm"], q + 1)
                for k in range(2):
                    ins = tt(t[:, k], bank(2 + q % 2, 2, TOK), tables[:, 1 - k, q:q + 1, :].broadcast_to([P, 2, TOK]),
                             ALU.mult)
                    c.then(ins, "bu_used")
                c.inc(tt(t[:, 0, 0], t[:, 0, 0], t[:, 1, 1], ALU.add), step)
                c.then(tt(t[:, 1, 0], t[:, 1, 0], t[:, 0, 1], ALU.subtract), step)
                if q >= 2:
                    dve.wait_ge(s["q_ready"], 2 * (q - 1))
                for k in range(2):
                    c.inc(v.tensor_tensor_scan(zz[:, q % 2, k], prm[:, MAG, q:q + 1].broadcast_to([P, TOK]), t[:, k, 0],
                                               0.0, ALU.mult, ALU.add), "z_ready")
                if q % 2 == 0 and q >= 2:
                    mods(4 + q // 2 - 1)
                if q in (6, 10, 14):
                    skip((q - 6) // 4)
                dve.wait_ge(s["z_ready"], 2 * (q + 1))
            mods(NADA - 1)
            skip(3)
            gate_cols(1, mod[:, 0, 2], norm_col(0, 1))
            for m in range(4):
                dve.wait_ge(s["glu_sig"], m + 1)
                c.inc(tt(yT[:, 4 + m], ys[:, m], uT[:, m], ALU.mult), "yT_ready")
            residual(1, 6, 2, grow)
            norm_x(xn, 3)
            scale_cols(2, NADA, mod[:, 0, 4], norm_col(0, 2))
            hT_low(2, mod[:, 0, 3])
            gate_cols(2, mod[:, 0, 5], norm_col(0, 3))

            for t in range(6):
                for j in range(2 if t == 5 else 4):
                    n = 4 * t + j
                    if j == 0 and t >= 2:
                        dve.wait_ge(s["tile_used"], AT["down", t - 2] + 1)
                    dve.wait_ge(s["f_mm"], 2 * n + 2)
                    dve.wait_ge(s["f_silu"], n + 1)
                    c.inc(tt(act_f[:, t % 2, j], silu_f[:, n % 2], ps[5][:, 0:TOK], ALU.mult), "f_act")
                if t:
                    mods(NADA + 2 * t - 1)
                mods(NADA + 2 * t)
            mods(2 * NADA - 1)
            residual(2, 12, 4, grow)

            norm_x(xn, 5)
            scale_cols(3, 2 * NADA, mod[:, 1, 1], norm_col(1, 0))
            hT_low(3, mod[:, 1, 0])
            gate_cols(3, mod[:, 1, 2], norm_col(1, 1))
            dve.wait_ge(s["l1_in"], 96)
            dve.wait_ge(s["dt_mm"], 1)
            dt_bias = bro[:, 0:HEADS].unsqueeze(1).broadcast_to([P, NB, HEADS])
            c.then(tt(hd[:, DA], bank(6, NB, HEADS), dt_bias, ALU.add), step)
            c.inc(stt(hd[:, TMP0], hd[:, DA], -1.0, hd[:, DA], ALU.mult, ALU.min), "dt_pre")
            c.inc(ts(hd[:, DT], hd[:, DA], 0.0, None, ALU.max), step)
            dve.wait_ge(s[step], c.n[step])
            dve.wait_ge(s["dt_ln"], 1)
            dve.wait_ge(s["a_exp"], 1)
            c.then(tt(hd[:, DT], hd[:, DT], hd[:, TMP0], ALU.add), step)
            c.then(stt(hd[:, DA], hd[:, DT], -1.0, hd[:, TMP1, 0:1].broadcast_to([P, NB, HEADS]), ALU.mult, ALU.mult),
                   "da_ready")
            for n in range(32):
                dve.wait_ge(s["xbc_mm"], n + 1)
                if n >= 2:
                    dve.wait_ge(s["silu_done"], n - 1)
                y, p = conv[:, n % 2], ps[n % 4]

                def tap(k):
                    return cols[:, 2, 32 * k + n:32 * k + n + 1]
                c.then(ts(y, p[:, 0:TOK], tap(3), cols[:, 1, C_CONVB + n:C_CONVB + n + 1], ALU.mult, ALU.add), step)
                for k in (2, 1):
                    c.then(stt(y[:, 3 - k:TOK], p[:, 0:TOK - 3 + k], tap(k), y[:, 3 - k:TOK], ALU.mult, ALU.add), step)
                c.inc(stt(y[:, 3:TOK], p[:, 0:TOK - 3], tap(0), y[:, 3:TOK], ALU.mult, ALU.add), "conv_done")

            def mixed(n):
                blk, grp = n // NG, n % NG
                dve.wait_ge(s["dec_exp"], n + 1)
                if n >= 2:
                    dve.wait_ge(s["y1_mm"], n - 1)
                c.inc(tt(mix[:, n % 2].rearrange("p (j l) -> p j l", j=4), dmin[:, n % 2].rearrange("p (j l) -> p j l", j=4),
                         cbm[:, n % 2:n % 2 + 1].broadcast_to([P, 4, P]), ALU.mult), "m_ready")
                if blk == 0:
                    dve.wait_ge(s["xdt_ready"], 2 * n + 1)
                    if n >= 2:
                        dve.wait_ge(s["st_mm"], n - 1)
                    c.inc(tt(xw[:, n % 2].rearrange("p (j c) -> p j c", j=4),
                             xdt[:, n % 2].rearrange("p (j c) -> p j c", j=4),
                             hd[:, TOEND, 0, 4 * grp:4 * grp + 4].unsqueeze(2).broadcast_to([P, 4, 64]), ALU.mult), "xw_ready")

            def gated(n):
                blk, grp = n // NG, n % NG
                bk = ps[3 + 2 * (n % 2)]
                o = yo[:, n % 2]
                dve.wait_ge(s["y1_mm"], n + 1)
                dve.wait_ge(s["xdt_ready"], 2 * n + 2)
                if blk:
                    c.then(tt(o.rearrange("p (j c) -> p j c", j=4), bk[:, TOK:HALF].rearrange("p (j c) -> p j c", j=4),
                              hd[:, ECS, 1, 4 * grp:4 * grp + 4].unsqueeze(2).broadcast_to([P, 4, 64]), ALU.mult), step)
                    c.then(tt(o, o, xd[:, n % 2], ALU.add), step)
                    c.then(tt(o, o, bk[:, 0:TOK], ALU.add), step)
                else:
                    c.then(tt(o, bk[:, 0:TOK], xd[:, n % 2], ALU.add), step)
                dve.wait_ge(s["z_silu"], 4 * blk + grp // 2 + 1)
                z = zs[:, blk, TOK * grp:TOK * grp + TOK]
                c.inc(tt(z, o, z, ALU.mult), "y_ready")
            dve.wait_ge(s["cs_exp"], 1)
            for n in range(NB * NG):
                dve.wait_ge(s["cb_mm"], n + 1)
                if n >= 2:
                    dve.wait_ge(s["m_ready"], n - 1)
                c.inc(tt(cbm[:, n % 2], ps[2][:, P * (n % 2):P * (n % 2) + P], tri[:, :], ALU.mult), "cbm_ready")
                dve.wait_ge(s["dec_mm"], n + 1)
                c.inc(ts(dmin[:, n % 2], ps[n % 2][:, :], 0.0, None, ALU.min), "dec_min")
                dve.wait_ge(s["cbm_ready"], n + 1)
                if n >= 1:
                    mixed(n - 1)
                if n >= 2:
                    gated(n - 2)
            mixed(NB * NG - 1)
            gated(NB * NG - 2)
            gated(NB * NG - 1)
            for m in range(0, 8, 2):
                dve.wait_ge(s["y_turned"], m + 1)
                for n in (2 * m, 2 * m + 1):
                    c.inc(ts(yT1[:, n], bank(m % 4, 2, TOK)[:, n % 2], cols[:, 1, C_M2G + n:C_M2G + n + 1], None, ALU.mult),
                          "yT1_a")
            root(6)
            c.inc(v.reciprocal(rst[:, 4:6], stat[:, 14:16]), "rg_ready")
            dve.wait_ge(s["rg_ready"], 1)
            residual(3, 20, 7, grow1, 4, True)

            scale_cols(4, 2 * NADA, mod[:, 1, 4], norm_col(1, 2))
            norm_x(xn2, 8)
            dve.wait_ge(s["row_ready"], 4)
            dve.wait_ge(s["xn_ready"], 8)
            for b in range(NB):
                c.then(tt(h_tok[:, b], xn2[:, b], gsrow, ALU.mult), step)
                c.inc(tt(h_tok[:, b], h_tok[:, b], shrow, ALU.add), "htok_ready")
            gate_cols(4, mod[:, 1, 5], norm_col(1, 3))
            dve.wait_ge(s["h2_turned"], 1)
            for i in (0, 1):
                c.inc(v.tensor_copy(hT2[:, 2 * i:2 * i + 2], bank(4 + i, 2, TOK)), "h2_low")
            c.inc(v.memset(acc, 0.0), "acc_zero")
            dve.wait_ge(s["logit_mm"], 1)
            r_bias = bro[:, 3 * HEADS:3 * HEADS + NE].unsqueeze(1).broadcast_to([P, NB, NE])
            c.then(tt(rt[:, LOGIT], bank(0, NB, NE), r_bias, ALU.add), step)
            c.then(v.tensor_reduce(rst[:, 6:8], rt[:, LOGIT], AX.X, ALU.max), step)
            c.inc(tt(rt[:, EXPS], rt[:, LOGIT], rst[:, 6:8].unsqueeze(2).broadcast_to([P, NB, NE]), ALU.subtract), "rt_pre")
            for b in range(NB):
                other = rt[:, LOGIT, b].unsqueeze(1).broadcast_to([P, NE, NE])
                own = rt[:, LOGIT, b].unsqueeze(2).broadcast_to([P, NE, NE])
                gt_, eq_ = (pair[:, i].rearrange("p (e f) -> p e f", e=NE) for i in range(2))
                c.inc(tt(gt_, other, own, ALU.is_gt), step)
                c.then(tt(eq_, other, own, ALU.is_equal), step)
                c.then(tt(eq_, eq_, earlier[:, :, :], ALU.mult), step)
                c.then(tt(gt_, gt_, eq_, ALU.add), step)
                c.then(v.tensor_reduce(rt[:, RANK, b], gt_, AX.X, ALU.add), step)
            c.then(ts(rt[:, SEL], rt[:, RANK], 2.0, None, ALU.is_lt), "mask_ready")
            dve.wait_ge(s["rt_exp"], 1)
            c.then(tt(rt[:, GATE], rt[:, EXPS], rt[:, SEL], ALU.mult), step)
            c.then(v.tensor_reduce(rst[:, 8:10], rt[:, GATE], AX.X, ALU.add), step)
            c.then(v.reciprocal(rst[:, 8:10], rst[:, 8:10]), step)
            c.then(tt(rt[:, GATE], rt[:, GATE], rst[:, 8:10].unsqueeze(2).broadcast_to([P, NB, NE]), ALU.mult), step)
            dve.wait_ge(s["pos_mm"], 1)
            c.then(stt(rt[:, POS], bank(1, NB, NE), 999.0, rt[:, SEL], ALU.add, ALU.mult), step)
            c.then(ts(rt[:, POS], rt[:, POS], -872.0, None, ALU.add), step)
            total = ps[1][0:1, 2 * NE:3 * NE]
            c.inc(ts(cnt_f[:, 0:NE], total, 1.0, None, ALU.max), step)
            c.then(ts(cnt_f[:, NE:2 * NE], total, -float(P), None, ALU.add), step)
            c.then(v.tensor_reduce(cnt_f[:, 16:17], cnt_f[:, NE:2 * NE], AX.X, ALU.max), step)
            c.inc(v.tensor_copy(cnt[:, :], cnt_f[:, :]), "cnt_ready")
            dve.wait_ge(s["cnt_ready"], 1)

            def prep(p):
                dve.wait_ge(s["tile_used"], p * (ITEM * NE) + MOE0)
                ts(rt[:, POS], rt[:, POS], -float(P), None, ALU.add).then_inc(s["pos_ready"], 1)
                past(dve, "pos_ready", p + 1)

                def scatter_rows(ep):
                    past(dve, "gT_mm", p * 4 + ep + 1)
                    v.tensor_copy(gT[:, 2 * ep:2 * ep + 2], bank(4, 2, TOK)).then_inc(s["gT_ready"], 1)
                for ep in range(4):
                    past(dve, "gather_mm", p * 4 + ep)
                    past(dve, "gT_mm", p * 4 + ep)
                    for b in range(NB):
                        for i in range(2):
                            e = 2 * ep + i
                            ts(hot[:, b, i], slot_iota[:, :], rt[:, POS, b, e:e + 1], None, ALU.is_equal)
                            ins = ts(hotg[:, b, i], slot_iota[:, :], rt[:, POS, b, e:e + 1], rt[:, GATE, b, e:e + 1],
                                     ALU.is_equal, ALU.mult)
                    ins.then_inc(s["hot_ready"], 1)
                    if ep == 0:
                        past(dve, "gcur_ready", p * NE)
                    if ep:
                        scatter_rows(ep - 1)
                scatter_rows(3)

            def item(p, e, k, nb):
                for t in range(4):
                    dve.wait_ge(s["tile_used"], k * ITEM + (MOE0 + DONE["u", t]))
                    past(dve, "e_silu", k * 4 + t + 1)
                    for b in range(nb):
                        w = WIDTHS[t]
                        ins = tt(sg[:, b, 0:w], sg[:, b, 0:w], ps[2 + b][:, 0:w], ALU.mult)
                    ins.then_inc(s["e_act"], 1)
                dve.wait_ge(s["tile_used"], k * ITEM + (MOE0 + ITEM))
                for b in range(nb):
                    ins = v.tensor_copy(y_sb[64 * b:64 * b + 64, HALF:D], ps[4 + b][64:128, :])
                ins.then_inc(s["y_high"], 1)
                past(dve, "acc_done", k * 4)
                for i in range(4):
                    o = acc[:, i // 2, HALF * (i % 2):HALF * (i % 2) + HALF]
                    past(dve, "scat_mm", k * 4 + i + 1)
                    tt(o, o, ps[6 + i % 2][:, :], ALU.add).then_inc(s["acc_done"], 1)
            dve.wait_ge(s["acc_zero"], 1)
            items = items_loop(dve, "dve", prep, item, True)
            past(dve, "acc_done", dve.snap(items) * 4)
            for b in range(NB):
                c.inc(v.tensor_tensor_reduce(tmp2[:, b], acc[:, b], acc[:, b], 1.0, 0.0, ALU.mult, ALU.add,
                                             stat[:, 8 + b:9 + b]), step)
            dve.wait_ge(s[step], c.n[step])
            c.inc(ts(stat[:, 8:10], stat[:, 8:10], 1.0, None, ALU.mult), "last_sum")
            dve.wait_ge(s["last_root"], 1)
            c.then(v.reciprocal(rst[:, 2:4], stat[:, 10:12]), step)
            dve.wait_ge(s["last_mm"], 1)
            for b in range(NB):
                for h in range(2):
                    at = slice(HALF * h, HALF * h + HALF)
                    c.inc(stt(tmp2[:, b, at], acc[:, b, at], rst[:, 2 + b:3 + b], ps[h][:, :], ALU.mult, ALU.mult), step)
                dve.wait_ge(s[step], c.n[step])
                c.inc(tt(x[:, b], x[:, b], tmp2[:, b], ALU.add), "final")

        @block.tensor
        def _(pe):
            mm, turn = nc.tensor.matmul, nc.tensor.transpose

            def arrived(i):
                pe.wait_ge(ring_full[TILES[i][2]], 16 * FILL[i])
                return TILES[i][2]

            def chain(out_, pairs, **kw):
                for i, (l, r) in enumerate(pairs):
                    ins = mm(out_, l, r, start=i == 0, stop=i == len(pairs) - 1, **kw)
                return ins

            def ada_mm(i):
                if i:
                    pe.wait_ge(s["ada_copied"], i)
                w = slot(arrived(ADA[i]), KC, HALF)
                for half in range(2):
                    for j in range(4):
                        kc = 2 * j + half
                        ins = mm(ps[6][32 * j:32 * j + 32, :], cT[:, kc, :], w[:, kc, :], start=half == 0, stop=half == 1)
                ins.then_inc(s["tile_used"], 1)

            def ada_turn(i):
                pe.wait_ge(s["ada_copied"], i + 1)
                if i:
                    pe.wait_ge(s["mod_ready"], i)
                for k in range(4):
                    ins = turn(ps[7][:, P * k:P * k + P], modpart[:, P * k:P * k + P], ident[:, :])
                ins.then_inc(s["ada_turned"], 1)

            def turn_x(src, name, base=0):
                for kc in range(KC):
                    for b in range(NB):
                        ins = turn(ps[base + kc // 2][:, TOK * (kc % 2) + P * b:TOK * (kc % 2) + P * b + P],
                                   src[:, b, P * kc:P * kc + P], ident[:, :])
                ins.then_inc(s[name], 1)

            def row_products(col, base):
                for kc in range(KC):
                    ins = mm(ps[base + kc // 4][:, P * (kc % 4):P * (kc % 4) + P], col[:, kc:kc + 1].broadcast_to([P, P]),
                             ident[:, :], start=True, stop=True)
                return ins

            pe.wait_ge(s["consts"], 2)
            pe.wait_ge(s["small_in"], 160)
            for i in range(3):
                ins = turn(ps[0][:, P * i:P * i + P], rows[:, i, :], ident[:, :])
            ins.then_inc(s["rows_turned"], 1)
            pe.wait_ge(s["s5_in"], 112)
            for i in range(2):
                for m in range(4):
                    ins = turn(ps[2 + i][:, P * m:P * m + P], c_raw[:, i, m], ident[:, :])
            ins.then_inc(s["c_turned"], 1)
            pe.wait_ge(s["c_ready"], 1)
            ada_mm(0)
            ada_turn(0)
            ada_mm(1)
            ada_turn(1)
            ada_mm(2)
            pe.wait_ge(s["xn_ready"], 2)
            pe.wait_ge(s["cols_ready"], 1)
            pe.wait_ge(s["ct_ready"], 24)
            turn_x(xn, "turned")
            ada_turn(2)
            ada_mm(3)
            ada_turn(3)
            for i in range(8):
                if i == 0:
                    pe.wait_ge(s["bx_ready"], 8)
                if i >= 2:
                    pe.wait_ge(s["bt_ready"], i - 1)
                for k in range(4):
                    ins = turn(ps[4 + i % 2][:, P * k:P * k + P], bx[:, k % 2, 2 * i + k // 2], ident[:, :])
                ins.then_inc(s["b_turned"], 1)

            pe.wait_ge(s["hT_low"], 4)
            pe.wait_ge(s["hT_high"], 4)
            pe.wait_ge(s["bt_ready"], 8)
            w = slot(arrived(AT["mixin", 0]), KC, HALF)
            for b in range(NB):
                ins = chain(ps[4 + b][:, :], [(hT[:, kc, P * b:P * b + P], w[:, kc]) for kc in range(KC)])
            ins.then_inc(s["tile_used"], 1)
            w = slot(arrived(AT["mixin", 1]), KC, HALF)
            for m in range(4):
                ins = chain(ps[m // 2][:, TOK * (m % 2):TOK * (m % 2) + TOK],
                            [(w[:, kc, P * m:P * m + P], hT[:, kc]) for kc in range(KC)])
            ins.then_inc(s["tile_used"], 1)
            pe.wait_ge(s["u_ready"], 4)
            pe.wait_ge(s["band_ready"], 6)
            pe.wait_ge(s["pw_in"], 16)
            for i in range(4):
                if i >= 2:
                    pe.wait_ge(s["pool_out"], i - 1)
                chain(ps[i % 2][:, 0:TOK], [(u_tok[:, b, P * i:P * i + P], band[:, i, b]) for b in range(NB)])\
                    .then_inc(s["pool_mm"], 1)
                pe.wait_ge(s["pool_in_ready"], i + 1)
                chain(ps[i % 2][:, TOK:HALF], [(pw[:, i], pool_in[:, i % 2])]).then_inc(s["pool_out_mm"], 1)

            def s5_out(q):
                pe.wait_ge(s["q_ready"], 2 * q + 2)
                m = q // 4
                if q % 4 == 0 and m >= 2:
                    pe.wait_ge(s["yskip"], m - 1)
                z = qq[:, q % 2]
                for i, (k, r) in enumerate(((0, z[:, 0, 0]), (0, z[:, 1, 1]), (2, z[:, 1, 0]), (1, z[:, 0, 1]))):
                    ins = mm(ps[4 + m % 2][:, 0:TOK], ct[:, q, k], r, start=q % 4 == 0 and i == 0,
                             stop=q % 4 == 3 and i == 3)
                ins.then_inc(s["y_mm"], 1)
            for q in range(NQ):
                if q >= 2:
                    pe.wait_ge(s["bu_used"], 2 * (q - 1))
                for k in range(2):
                    ins = mm(ps[2 + q % 2][:, TOK * k:TOK * k + TOK], bt[:, q, k], uT[:, q // 4], start=True, stop=True)
                ins.then_inc(s["bu_mm"], 1)
                if q % 2 == 0 and q >= 2:
                    ada_turn(4 + q // 2 - 1)
                if q >= 2:
                    s5_out(q - 2)
                if q % 2:
                    ada_mm(4 + q // 2)
            ada_turn(NADA - 1)
            s5_out(NQ - 2)
            s5_out(NQ - 1)
            pe.wait_ge(s["ys_ready"], 4)
            pe.wait_ge(s["pool_out"], 4)
            pe.wait_ge(s["bu_used"], 2 * NQ)
            w = slot(arrived(AT["glu", 0]), 4, HALF)
            for m in range(4):
                chain(ps[m][:, 0:TOK], [(w[:, k, P * m:P * m + P], ys[:, k]) for k in range(4)]).then_inc(s["glu_mm"], 1)
            pe.wait_ge(s["gg_ready"], 1)
            pe.wait_ge(s["yskip"], 4)
            row_products(gg, 4).then_inc(s["grow_mm"], 1)
            pe.wait_ge(s["yT_ready"], 4)
            pe.wait_ge(s["glu_sig"], 4)
            pe.wait_ge(s["glu_mm"], 4)
            for h in range(2):
                i = AT["mixout", h]
                w = slot(arrived(i), KC, HALF)
                if h == 0:
                    pe.sem_inc(s["tile_used"], 1)
                for b in range(NB):
                    ins = chain(ps[2 * b + h][:, :], [(yT[:, kc, P * b:P * b + P], w[:, kc]) for kc in range(KC)])
                ins.then_inc(s["tile_used"], 1)

            pe.wait_ge(s["x_ready"], 2)
            pe.wait_ge(s["xn_ready"], 4)
            turn_x(xn, "turned")
            pe.wait_ge(s["hT_low"], 8)
            pe.wait_ge(s["hT_high"], 8)
            pe.wait_ge(s["grow_ready"], 2)

            def ffn_down(t):
                n = 2 if t == 5 else 4
                w = slot(arrived(AT["down", t]), n, D)
                for j in range(n):
                    pe.wait_ge(s["f_act"], 4 * t + j + 1)
                    for b in range(NB):
                        for h in range(2):
                            ins = mm(ps[2 * b + h][:, :], act_f[:, t % 2, j, P * b:P * b + P], w[:, j, HALF * h:HALF * h + HALF],
                                     start=t == 0 and j == 0, stop=t == 5 and j == n - 1)
                ins.then_inc(s["tile_used"], 1)
            for t in range(6):
                n_f = 2 if t == 5 else 4
                g, u = AT["gate", t], AT["up", t]
                wg = slot(arrived(g), KC, P * n_f)
                wu = slot(arrived(u), KC, P * n_f)
                for j in range(n_f):
                    n = 4 * t + j
                    for k, w in enumerate((wg, wu)):
                        if n:
                            pe.wait_ge(s["f_act" if k else "f_silu"], n)
                        ins = chain(ps[4 + k][:, 0:TOK],
                                    [(w[:, kc, P * j:P * j + P], hT[:, kc]) for kc in range(KC)])
                        ins.then_inc(s["f_mm"], 1)
                if t:
                    ada_turn(NADA + 2 * t - 1)
                pe.wait_ge(s["f_mm"], 8 * t + 2 * n_f)
                pe.sem_inc(s["tile_used"], 2)
                ada_mm(NADA + 2 * t)
                if t:
                    ffn_down(t - 1)
                ada_turn(NADA + 2 * t)
                ada_mm(NADA + 2 * t + 1)
            pe.wait_ge(s["gg_ready"], 2)
            pe.wait_ge(s["f_act"], 22)
            row_products(gg, 4).then_inc(s["grow_mm"], 1)
            ada_turn(2 * NADA - 1)
            ffn_down(5)

            pe.wait_ge(s["x_ready"], 4)
            pe.wait_ge(s["xn_ready"], 6)
            turn_x(xn, "turned")
            pe.wait_ge(s["hT_low"], 12)
            pe.wait_ge(s["hT_high"], 12)
            pe.wait_ge(s["l1_in"], 96)
            pe.wait_ge(s["ada_copied"], 2 * NADA)
            for b in range(NB):
                ins = chain(ps[6][:, HEADS * b:HEADS * b + HEADS],
                            [(hT[:, kc, P * b:P * b + P], dtw[:, kc, :]) for kc in range(KC)])
            ins.then_inc(s["dt_mm"], 1)

            def turn_conv(n):
                pe.wait_ge(s["silu_done"], n + 1)
                if n < 16:
                    m = n // 2
                    if n % 2 == 0 and m >= 2:
                        pe.wait_ge(s["xs_ready"], m - 1)
                    for b in range(NB):
                        at = TOK * b + P * (n % 2)
                        ins = turn(ps[4 + m % 2][:, at:at + P], xsT[:, n % 2, P * b:P * b + P], ident[:, :])
                    ins.then_inc(s["xs_turned"], 1)
                else:
                    g = n - 16
                    if g % 4 == 0:
                        pe.wait_ge(s["xs_ready"], 7 + g // 4)
                    turn(ps[4 + g // 4][:, P * (g % 4):P * (g % 4) + P], bc[:, 0, g, 0:P], ident[:, :])\
                        .then_inc(s["b_turned1"], 1)
            pe.wait_ge(s["grow_ready"], 4)
            for n in range(32):
                i = AT["xbc", n // 4]
                if n % 4 == 0:
                    w = slot(arrived(i), KC, HALF)
                if n >= 4:
                    pe.wait_ge(s["conv_done"], n - 3)
                ins = chain(ps[n % 4][:, 0:TOK], [(w[:, kc, P * (n % 4):P * (n % 4) + P], hT[:, kc]) for kc in range(KC)])
                ins.then_inc(s["xbc_mm"], 1)
                if n % 4 == 3:
                    pe.wait_ge(s["xbc_mm"], n + 1)
                    pe.sem_inc(s["tile_used"], 1)
                if 2 <= n < 26:
                    turn_conv(n - 2)
                if n == 4:
                    pe.wait_ge(s["consts"], 12)
                    pe.wait_ge(s["da_ready"], 1)
                    for k, m in enumerate((tri, after)):
                        for b in range(NB):
                            at = P + 2 * HEADS * k + HEADS * b
                            ins = mm(ps[6][:, at:at + HEADS], m[:, :], hd[:, DA, b], start=True, stop=True)
                    ins.then_inc(s["cs_mm"], 1)

            def z_part(n):
                zi = n // 2
                b, sl = zi // 4, zi % 4
                if n % 2 == 0:
                    if zi >= 2:
                        pe.wait_ge(s["z_silu"], zi - 1)
                    if zi < 4:
                        arrived(AT["z", sl])
                w = slot(TILES[AT["z", sl]][2], KC, HALF)
                for kc in range(4 * (n % 2), 4 * (n % 2) + 4):
                    ins = mm(ps[6 + zi % 2][:, :], hT[:, kc, P * b:P * b + P], w[:, kc], start=kc == 0, stop=kc == KC - 1)
                if n % 2:
                    ins.then_inc(s["z_mm"], 1)
                    if b == 1:
                        pe.wait_ge(s["z_mm"], zi + 1)
                        pe.sem_inc(s["tile_used"], 1)

            def y_products(n):
                blk, grp = n // NG, n % NG
                bk = ps[3 + 2 * (n % 2)]
                pe.wait_ge(s["m_ready"], n + 1)
                pe.wait_ge(s["xdt_ready"], 2 * n + 1)
                if n >= 2:
                    pe.wait_ge(s["y_ready"], n - 1)
                for j in range(4):
                    ins = mm(bk[:, 64 * j:64 * j + 64], mix[:, n % 2, P * j:P * j + P], xdt[:, n % 2, 64 * j:64 * j + 64],
                             start=True, stop=True)
                if blk:
                    pe.wait_ge(s["st_ready"], grp + 1)
                    ins = mm(bk[:, TOK:HALF], bc[:, 1, grp, P:TOK], st[:, grp], start=True, stop=True)
                ins.then_inc(s["y1_mm"], 1)
                if blk == 0:
                    pe.wait_ge(s["xw_ready"], n + 1)
                    if n:
                        pe.wait_ge(s["st_ready"], n)
                    mm(ps[4][:, TOK * (n % 2):TOK * (n % 2) + TOK], btok[:, grp], xw[:, n % 2], start=True, stop=True)\
                        .then_inc(s["st_mm"], 1)
            pe.wait_ge(s["silu_done"], 32)
            pe.wait_ge(s["conv_done"], 32)
            pe.wait_ge(s["btok_ready"], 2)
            pe.wait_ge(s["cs_exp"], 1)
            for n in range(NB * NG):
                blk, grp = n // NG, n % NG
                if n >= 2:
                    pe.wait_ge(s["dec_min"], n - 1)
                da = hd[:, DA, blk, 4 * grp:4 * grp + 4]
                dec = bank(n % 2, 4, P)
                mm(dec, ntri[:, :], da.unsqueeze(2).broadcast_to([P, 4, P]), start=True, stop=False, skip_group_check=True)
                for j in range(4):
                    ins = mm(dec[:, j], da[:, j:j + 1].broadcast_to([P, P]), tri[:, :], start=False, stop=j == 3,
                             skip_group_check=True)
                ins.then_inc(s["dec_mm"], 1)
                if n:
                    pe.wait_ge(s["cbm_ready"], n)
                mm(ps[2][:, P * (n % 2):P * (n % 2) + P], bc[:, 0, grp, P * blk:P * blk + P], bc[:, 1, grp, P * blk:P * blk + P],
                   start=True, stop=True).then_inc(s["cb_mm"], 1)
                z_part(n)
                if n:
                    y_products(n - 1)
            y_products(NB * NG - 1)
            pe.wait_ge(s["dec_min"], NB * NG)
            pe.wait_ge(s["gg_ready"], 3)
            row_products(gg, 0).then_inc(s["grow_mm"], 1)
            pe.wait_ge(s["grow_ready"], 6)
            pe.wait_ge(s["cbm_ready"], NB * NG)
            pe.wait_ge(s["y_ready"], NB * NG)
            for n in range(16):
                m = n // 2
                if n % 2 == 0 and m >= 4:
                    pe.wait_ge(s["yT1_b" if m % 2 else "yT1_a"], 2 * ((m - 4) // 2) + 2)
                for b in range(NB):
                    at = TOK * (n % 2) + P * b
                    ins = turn(ps[m % 4][:, at:at + P], zs[:, b, P * n:P * n + P], ident[:, :])
                if n % 2:
                    ins.then_inc(s["y_turned"], 1)
            pe.wait_ge(s["st_ready"], NG)
            pe.wait_ge(s["z_silu"], 8)
            for n in range(16):
                if n % 4 == 0:
                    w = slot(arrived(AT["m2out", n // 4]), 4, D)
                pe.wait_ge(s["yT1_b" if n // 2 % 2 else "yT1_a"], 2 * (n // 4) + n % 2 + 1)
                for b in range(NB):
                    for h in range(2):
                        ins = mm(ps[4 + 2 * b + h][:, :], yT1[:, n, P * b:P * b + P], w[:, n % 4, HALF * h:HALF * h + HALF],
                                 start=n == 0, stop=n == 15)
                if n % 4 == 3:
                    ins.then_inc(s["tile_used"], 2 if n == 15 else 1)

            pe.wait_ge(s["yT1_a"], 8)
            pe.wait_ge(s["yT1_b"], 8)
            pe.wait_ge(s["gs_ready"], 4)
            row_products(gs, 0)
            row_products(mod[:, 1, 3], 2).then_inc(s["row_mm"], 1)
            pe.wait_ge(s["htok_ready"], 2)
            pe.wait_ge(s["x_ready"], 6)
            turn_x(h_tok, "h2_turned", 4)
            pe.wait_ge(s["h2_low"], 2)
            pe.wait_ge(s["h2_high"], 2)
            pe.wait_ge(s["row_ready"], 4)
            for b in range(NB):
                ins = chain(ps[0][:, NE * b:NE * b + NE], [(hT2[:, kc, P * b:P * b + P], rw[:, kc, :]) for kc in range(KC)])
            ins.then_inc(s["logit_mm"], 1)
            pe.wait_ge(s["mask_ready"], 1)
            sel = rt[:, SEL]
            chain(ps[1][:, 0:NE], [(tri[:, :], sel[:, 0])])
            chain(ps[1][:, NE:2 * NE], [(tri[:, :], sel[:, 1]), (ones[:, :], sel[:, 0])])
            chain(ps[1][:, 2 * NE:3 * NE], [(ones[:, :], sel[:, 0]), (ones[:, :], sel[:, 1])]).then_inc(s["pos_mm"], 1)

            def prep(p):
                for ep in range(4):
                    past(pe, "hot_ready", p * 4 + ep + 1)
                    past(pe, "hg_ready", p * 16 + 4 * ep)
                    for kc in range(KC):
                        at = TOK * (kc % 2)
                        ins = chain(ps[kc // 2][:, at:at + TOK],
                                    [(h_tok[:, b, P * kc:P * kc + P], hot[:, b].rearrange("p e n -> p (e n)")) for b in range(NB)])
                    ins.then_inc(s["gather_mm"], 1)
                    past(pe, "gT_ready", p * 4 + ep)
                    for i in range(2):
                        for b in range(NB):
                            at = TOK * i + P * b
                            ins = turn(ps[4][:, at:at + P], hotg[:, b, i], ident[:, :])
                    ins.then_inc(s["gT_mm"], 1)

            def item(p, e, k, nb):
                fill = [k * 48 + 16 * FILLS0[i] for i in range(RING)]

                def expert_tile(what, t, h):
                    j = FIRST[what, t] + h
                    pe.wait_ge(ring_full[j % RING], fill[j % RING] + 16 * (j // RING + 1))
                    return j % RING

                def hidden(what, t, base):
                    w = WIDTHS[t]
                    if t < 3:
                        sl = [slot(expert_tile(what, t, h), KC, HALF) for h in range(2)]
                        wt = [sl[h][:, :, :] for h in range(2)]
                    else:
                        one = slot(expert_tile(what, t, 0), KC, HALF)
                        wt = [one[:, :, w * h:w * h + w] for h in range(2)]
                    for b in range(nb):
                        for kc in range(KC):
                            for h in range(2):
                                ins = mm(ps[base + b][64 * h:64 * h + 64, 0:w], hcur3[:, kc, 64 * b:64 * b + 64], wt[h][:, kc],
                                         start=kc == 0, stop=kc == KC - 1)
                    ins.then_inc(s["tile_used"], 2 if t < 3 else 1)

                def turn_hidden(t):
                    past(pe, "e_act", k * 4 + t + 1)
                    past(pe, "actT_ready", k * 4 + t)
                    if t == 0:
                        past(pe, "acc_done", k * 4)
                    for b in range(nb):
                        for i in range(WIDTHS[t] // P):
                            ins = turn(ps[6 + b][:, P * i:P * i + P], sg[:, b, P * i:P * i + P], ident[:, :])
                    ins.then_inc(s["e_turned"], 1)

                def output(t):
                    past(pe, "actT_ready", k * 4 + t + 1)
                    n = WIDTHS[t] // P
                    if t == 0:
                        past(pe, "y_low", k)
                        past(pe, "y_high", k)
                    sl = [slot(expert_tile("d", t, h), 4, D) for h in range(2 if t < 3 else 1)]
                    for b in range(nb):
                        for half in range(2):
                            for i in range(n):
                                row = half * n + i
                                for h in range(2):
                                    ins = mm(ps[4 + b][64 * h:64 * h + 64, :], actT[:, t % 2, b, i, 64 * half:64 * half + 64],
                                             sl[row // 4][:, row % 4, HALF * h:HALF * h + HALF],
                                             start=t == 0 and row == 0, stop=t == 3 and row == 2 * n - 1)
                    ins.then_inc(s["tile_used"], 2 if t < 3 else 1)
                past(pe, "hcur_ready", k + 1)
                past(pe, "gT_ready", p * 4 + 4)
                for t in range(4):
                    past(pe, "e_silu", k * 4 + t)
                    hidden("g", t, 0)
                    if t:
                        turn_hidden(t - 1)
                    past(pe, "e_act", k * 4 + t)
                    hidden("u", t, 2)
                    if t:
                        output(t - 1)
                turn_hidden(3)
                output(3)
                past(pe, "y_low", k + 1)
                past(pe, "y_high", k + 1)
                past(pe, "gcur_ready", k + 1)
                for i in range(4):
                    if i >= 2:
                        past(pe, "acc_done", k * 4 + i - 1)
                    mm(ps[6 + i % 2][:, :], gcur[0:64 * nb, P * (i // 2):P * (i // 2) + P],
                       y_sb[0:64 * nb, HALF * (i % 2):HALF * (i % 2) + HALF], start=True, stop=True).then_inc(s["scat_mm"], 1)
            items = items_loop(pe, "pe", prep, item, True)
            past(pe, "e_silu", pe.snap(items) * 4)
            pe.wait_ge(s["gg_ready"], 4)
            row_products(gg, 0).then_inc(s["last_mm"], 1)


_INS = ["x", "c", "ada_w", "ada_b", "norm_g", "mix_w_in", "pool_w", "pool_scale", "s5_lam_re", "s5_lam_im",
        "s5_log_step", "s5_b_re", "s5_b_im", "s5_c_re", "s5_c_im", "s5_d", "s5_w_glu", "mix_w_out",
        "ffn_w_gate", "ffn_w_up", "ffn_w_down", "m2_w_in", "m2_conv_w", "m2_conv_b", "m2_dt_bias", "m2_a_log",
        "m2_d", "m2_norm_g", "m2_w_out", "moe_w_router", "moe_b_router", "moe_w_gate", "moe_w_up", "moe_w_down"]


def kernel(**inputs):
    import numpy as _np
    import concourse.bacc as _bacc
    from concourse import mybir as _mybir
    from concourse.bass_utils import run_bass_kernel_spmd as _run

    nc = _bacc.Bacc("TRN2", target_bir_lowering=False, num_devices=1)
    arrays, aps = {}, {}
    for name in _INS:
        v = _np.ascontiguousarray(inputs[name])
        arrays[f"in_{name}"] = v
        aps[name] = nc.dram_tensor(f"in_{name}", v.shape, _mybir.dt.from_np(v.dtype), kind="ExternalInput").ap()
    out = nc.dram_tensor("out", (1, TOK, D), F32, kind="ExternalOutput").ap()
    hybrid_trunk(nc, aps, out)
    r = _run(nc, [arrays], core_ids=[0])
    return r.results[0]["out"]
```

```python
from contextlib import ExitStack

import concourse.bass as bass
from concourse import mybir

ALU = mybir.AluOpType
ACT = mybir.ActivationFunctionType
AX = mybir.AxisListType
F32 = mybir.dt.float32
I32 = mybir.dt.int32

P = 128
D = 1024
KC = D // P
TOK = 256
NB = TOK // P
EPS = 1e-6
HALF = 512
NADA = 6 * D // HALF
POOL_WINDOWS = (2, 4, 8, 16)
NQ = 16
FFN = 2816
INNER = 2048
HEADS = 32
NG = 8
NE = 8
EH = 3584
RING = 7
WARM_ROWS, WARM_C, WARM_NORM, WARM_ADA, WARM_GATHER, WARM_ITEM = 36, 20, 16, 13, 8, 8
TILE = 4096
S5_SLOTS = 4
L1_SLOTS = 6
ROUND = 12582912.0
TWO_PI = 6.283185
INV_TWO_PI = 0.15915494309189535
WIDTHS = (512, 512, 512, 256)
ITEM = 21


def plan():
    tiles = []

    def put(kind, n, slot):
        tiles.append((kind, n, slot))

    head = [("ada0", n) for n in range(4)] + [("mixin", 0), ("mixin", 1)]
    head += [("ada0", n) for n in range(4, NADA)] + [("glu", 0), ("mixout", 0), ("mixout", 1)]
    for n, (kind, i) in enumerate(head):
        put(kind, i, n % S5_SLOTS)
    ada = [("ada1", n) for n in range(NADA)]
    ffn = ada[:2]
    for t in range(6):
        ffn += [("gate", t), ("up", t)]
        if t < 4:
            ffn.append(ada[2 * t + 2])
        if t:
            ffn.append(("down", t - 1))
        if t < 4:
            ffn.append(ada[2 * t + 3])
    ffn += [("down", 5)] + ada[10:]
    for n, (kind, i) in enumerate(ffn):
        put(kind, i, (n + 4) % RING)
    l1 = [("xbc", n) for n in range(8)] + [("z", n) for n in range(4)] + [("m2out", n) for n in range(4)]
    for n, (kind, i) in enumerate(l1):
        put(kind, i, (n - len(l1)) % L1_SLOTS)
    return tiles


TILES = plan()
NTILES = len(TILES)
AT = {(kind, n): i for i, (kind, n, _) in enumerate(TILES)}
ADA = [AT[f"ada{i // NADA}", i % NADA] for i in range(2 * NADA)]
LAST_SLOT6 = max(i for i, t in enumerate(TILES) if t[2] == 6)
MOE0 = NTILES + 1
FILL, LAST_USER = [], []
_fills, _user = [0] * RING, [None] * RING
for _i, (_k, _n, _s) in enumerate(TILES):
    _fills[_s] += 1
    FILL.append(_fills[_s])
    LAST_USER.append(_user[_s])
    _user[_s] = _i
FILLS0 = list(_fills)
ORDER = []
for _t in range(4):
    _m = 2 if _t < 3 else 1
    ORDER += [("g", _t, _m), ("u", _t, _m)] + ([("d", _t - 1, 2)] if _t else [])
ORDER.append(("d", 3, 1))
FIRST, DONE = {}, {}
_at = 0
for _w, _t, _m in ORDER:
    FIRST[_w, _t] = _at
    _at += _m
    DONE[_w, _t] = _at
assert _at == ITEM and ITEM % RING == 0


def hybrid_trunk(nc, a, out):
    with ExitStack() as ctx:
        def sb(name, shape, dt=F32):
            return ctx.enter_context(nc.sbuf_tensor(name, shape, dt))

        def sem(name):
            return ctx.enter_context(nc.semaphore(name))

        ps = [ctx.enter_context(nc.psum_tensor(f"bank{i}", [P, HALF], F32)) for i in range(8)]

        ring = sb("ring", [P, RING, TILE])
        x = sb("x", [P, NB, D])
        ident = sb("ident", [P, P])
        tri = sb("tri", [P, P])
        ntri = sb("ntri", [P, P])
        after = sb("after", [P, P])
        ones = sb("ones", [P, P])
        slot_iota = sb("slot_iota", [P, P])
        earlier = sb("earlier", [P, NE, NE])
        cols = sb("cols", [P, 3, P])
        mod = sb("mod", [P, 2, 6, KC])
        mod_flat = mod[:, :, :, :].rearrange("p l v k -> p (l v k)")
        modraw = sb("modraw", [P, 2, 4])
        cT = sb("cT", [P, KC, 32])
        gs = sb("gs", [P, KC])
        gg = sb("gg", [P, KC])
        stat = sb("stat", [P, 16])
        rst = sb("rst", [P, 10])
        s5_tmp = sb("s5_tmp", [P, TOK])
        eps = sb("eps", [P, 1])
        dtw = sb("dtw", [P, KC, HEADS])
        rw = sb("rw", [P, KC, NE])
        bro = sb("bro", [P, 3 * HEADS + NE])
        hd = sb("hd", [P, 6, NB, HEADS])
        rt = sb("rt", [P, 6, NB, NE])
        cnt_f = sb("cnt_f", [1, 17])
        cnt = sb("cnt", [1, 17], I32)
        ARENA = 19456
        arena = sb("arena", [P, ARENA])

        def area(at, *shape):
            n = 1
            for s in shape:
                n *= s
            assert at + n <= ARENA, (at, n)
            v = arena[:, at:at + n]
            if len(shape) == 1:
                return v
            names = "abcd"[:len(shape)]
            return v.rearrange(f"p ({' '.join(names)}) -> p {' '.join(names)}",
                               **{k: s for k, s in zip(names, shape)})

        def slot(s, *shape):
            n = 1
            for k in shape:
                n *= k
            names = "abcd"[:len(shape)]
            return ring[:, s, 0:n].rearrange(f"p ({' '.join(names)}) -> p {' '.join(names)}",
                                             **{k: v for k, v in zip(names, shape)})

        def bank(i, *shape):
            n = 1
            for k in shape:
                n *= k
            names = "abcd"[:len(shape)]
            return ps[i][:, 0:n].rearrange(f"p ({' '.join(names)}) -> p {' '.join(names)}",
                                           **{k: v for k, v in zip(names, shape)})

        lam_re, lam_im = cols[:, 0, 96:112], cols[:, 0, 112:128]
        C_PSCALE, C_S5D, C_M2G, C_CONVB, C_C = 64, 68, 72, 88, 120

        def norm_col(layer, i):
            at = (layer * 4 + i) * KC
            return cols[:, 1, at:at + KC]

        tables = ring[:, 4:6, :].rearrange("p k (q t) -> p k q t", q=NQ)
        bt = slot(6, NQ, 2, P)
        rows = slot(3, 3, P)
        t_row = s5_tmp[:, :]
        inv_cnt = area(11264, 4, TOK)
        xn0 = area(0, NB, D)
        hT = area(0, KC, TOK)
        yT = area(0, KC, TOK)
        ct = area(2048, NQ, 2, P)
        band = area(8192, 4, NB, TOK)
        u_tok = area(10240, NB, HALF)
        uT = area(11264, 4, TOK)
        ys = area(12288, 4, TOK)
        b_raw, bb = area(10240, 2, NQ, 16), area(10752, 2, NQ, 16)
        c_raw = area(12288, 2, 4, P)
        grow = area(13312, D)
        modparts = area(13312, HALF), area(18944, HALF)
        temps = area(14336, 2, 2, 2, TOK)
        zz = area(16384, 2, 2, TOK)
        qq = area(17408, 2, 2, 2, TOK)
        xn = area(14336, NB, D)
        junk_sq = area(16384, 4, HALF)
        sqrt_table = sb("sqrt_table", [P, 4])
        OUT_ORDER = ((0, 2, 1, 3), (0, 1, 2, 3), (0, 1, 2, 3))
        tmp = area(14336, NB, D)
        bx = area(14336, 2, NQ, P)
        pw = area(18432, 4, P)
        pool_in = area(18944, 2, TOK)
        STEP, LRSTEP, MAG, LR, TAU, PA, FR, FI, PB, PC, INV, SIN1 = range(12)
        prm = hd[:, 0:3].rearrange("p a b c -> p (a b c)").rearrange("p (r q) -> p r q", q=NQ)
        log_step = prm[:, FR:FI + 1].rearrange("p a q -> p (a q)")
        act_f = area(2048, 2, 4, TOK)
        silu_f = area(4096, 2, TOK)
        xs = area(2048, NB, INNER)
        zs = area(6144, NB, INNER)
        bc = slot(6, 2, NG, TOK)
        btok = area(10240, NG, P)
        conv = area(12288, 2, TOK)
        xsT = area(12800, 2, TOK)
        dmin = area(13312, 2, HALF)
        mix = area(14336, 2, HALF)
        cbm = area(15360, 2, P)
        xdt = area(15616, 2, TOK)
        xw = area(12288, 2, TOK)
        xd = area(12800, 2, TOK)
        yo = area(16128, 2, TOK)
        st = area(16640, NG, TOK)
        junk_y = area(12288, INNER)
        yT1 = area(2048, 16, TOK)
        grow1 = area(11264, D)
        hot = area(2048, NB, P)
        hotg = area(2304, NB, P)
        slots_of = area(2560, 2, NE, NB * 3).rearrange("p q e (b i) -> p q e b i", i=3)
        slots_flat = area(2560, (2 * NE + 1) * NB * 3)
        pair = area(3840, 2, NB, NE * NE).rearrange("p i b (e f) -> p i b e f", e=NE)
        grow2 = area(2816, D)
        slots = area(2688, NB, 3)
        acc = area(12288, NB, D)
        hcur = area(14336, KC * P)
        hcur3 = area(14336, KC, P)
        gcur = dtw.rearrange("p a b -> p (a b)")
        sg = area(15360, 2, HALF)
        actT = area(16384, 2, 2, 4, P)
        y_sb = area(18432, D)
        hT2 = area(16384, KC, TOK)
        tmp2 = area(4096, NB, D)
        junk_acc = area(6144, NB, D)
        DT, DA, ECS, TOEND, TMP0, TMP1 = range(6)
        LOGIT, EXPS, SEL, GATE, POS, RANK = range(6)

        names = """small_in x_in s5_in pw_in l1_in consts t_iota rows_turned cols_ready cT_zero c_ready
            ada_copied ada_turned mod_ready inv_ready band_ready
            step_exp step_ready mag_ready inv_tail turn_ready turn_sin tab_ready tab_sin bx_zero bx_ready b_turned bt_ready c_turned ct_zero ct_ready
            xn_ready turned hT_low hT_high gs_ready u_ready pool_mm pool_in_ready pool_out_mm pool_out
            bu_mm bu_used z_ready q_ready re_ready im_ready y_mm yskip ys_ready glu_mm glu_sig yT_ready gg_ready grow_mm grow_ready
            sq_done rg_ready root_in root_done xroot_done out_mm x_ready dve_step             f_mm f_silu f_act
            dt_mm dt_pre dt_exp dt_ln a_exp da_ready cs_mm cs_exp
            xbc_mm conv_done silu_done xs_turned xs_ready b_turned1 btok_ready z_mm z_silu
            dec_mm dec_min dec_exp cb_mm cbm_ready m_ready xw_ready xdt_ready y1_mm st_mm st_ready y_ready
            y_turned yT1_a yT1_b logit_mm rt_pre rt_exp
            mask_ready pos_mm cnt_ready acc_zero slots_zero slots_ready hot_ready gather_mm hg_ready gT_mm gT_ready
            e_silu e_act e_turned actT_ready y_low y_high scat_mm acc_done
            last_scaled last_root final stored tile_used""".split()
        s = {n: sem(n) for n in names}
        ring_full = [sem(f"ring_full{i}") for i in range(RING)]
        block = ctx.enter_context(nc.Block())

        class Counted:

            def __init__(self, eng):
                self.eng, self.n = eng, {}

            def inc(self, ins, name):
                ins.then_inc(s[name], 1)
                self.n[name] = self.n.get(name, 0) + 1

            def then(self, ins, name):
                self.inc(ins, name)
                self.eng.wait_ge(s[name], self.n[name])

        def w_cols(w, at, n):
            return w.rearrange("(k p) n -> p k n", p=P)[:, :, at:at + n]

        def w_rows(w, at, n):
            return w[at:at + n * P, :].rearrange("(k p) n -> p k n", p=P)

        PRIMED = {"pe": ("gather_mm", "gT_mm", "e_turned", "scat_mm"), "act": ("e_silu", "actT_ready", "y_low"),
                  "dve": ("hg_ready", "gT_ready", "e_act", "y_high", "acc_done", "hot_ready"), "pool": ("slots_ready",)}

        def past(eng, name, n):
            eng.wait_ge(s[name], n + 1)

        SCATTER = (6, 7, 4, 5)

        def bank_columns(nb, m, w):
            per = 64 // m
            return [min(per, nb - at) * w // per for at in range(0, nb, per)]

        def output_parts(nb, m, half):
            parts, per, w = P // m, 64 // m, D * m // P
            return [(y_sb[m * b:m * b + m, w * q:w * q + w],
                     ps[4 + b // per][m * q:m * q + m, w * (b % per):w * (b % per) + w])
                    for b in range(nb) for q in range(half * parts // 2, (half + 1) * parts // 2)]

        def items_loop(eng, name, first, item, skipped, by_items=True):
            eng.wait_ge(s["cnt_ready"], 1)
            for primed in PRIMED[name]:
                eng.sem_inc(s[primed], 1)
            items = ctx.enter_context(eng.register(f"{name}_items"))
            eng.reg_mov(items, 0)
            first()
            with eng.Fori(0, 2) as p:
                run = eng.value_load(cnt[0:1, bass.ds(p * 16, 1)])
                with eng.If(run > 0):
                    with eng.Fori(0, NE) as e:
                        g = p * NE + e
                        if not by_items:
                            item(g)
                        else:
                            n = eng.value_load(cnt[0:1, bass.ds(p * NE + e, 1)])
                            with eng.If(n > 0):
                                k = eng.snap(items)
                                with eng.If(n > 96):
                                    item(g, k, 2, 64)
                                with eng.Else():
                                    with eng.If(n > 64):
                                        item(g, k, 3, 32)
                                    with eng.Else():
                                        item(g, k, 1, 64)
                                eng.reg_add(items, items, 1)
                            if skipped is not None:
                                with eng.Else():
                                    skipped(g, eng.snap(items))
            return items

        @block.sync
        def _(sp):
            def part(w, n, total):
                return w_cols(w, n * HALF, min(HALF, total - n * HALF)), KC, min(HALF, total - n * HALF)

            def down(n):
                k = min(4, (FFN - n * HALF) // P)
                return w_rows(a["ffn_w_down"][0], n * HALF, k), k, D
            sources = {
                "ada0": lambda n: part(a["ada_w"][0], n, 6 * D), "ada1": lambda n: part(a["ada_w"][1], n, 6 * D),
                "mixin": lambda n: part(a["mix_w_in"][0], n, D), "mixout": lambda n: part(a["mix_w_out"][0], n, D),
                "glu": lambda n: (w_cols(a["s5_w_glu"][0], 0, HALF), 4, HALF),
                "gate": lambda n: part(a["ffn_w_gate"][0], n, FFN), "up": lambda n: part(a["ffn_w_up"][0], n, FFN),
                "down": down,
                "xbc": lambda n: (w_cols(a["m2_w_in"][0], INNER + n * HALF, HALF), KC, HALF),
                "z": lambda n: (w_cols(a["m2_w_in"][0], n * HALF, HALF), KC, HALF),
                "m2out": lambda n: (w_rows(a["m2_w_out"][0], n * HALF, 4), 4, D),
            }
            def by_p(v):
                return v.rearrange("(r p) -> r p", p=P)

            def small(dst, src):
                sp.dma_start(dst, src).then_inc(s["small_in"], 16)
            small(rows[120:128, 1, :], by_p(a["c"][0]))
            small(rows[0:96, 0, :], a["ada_b"].rearrange("l (r p) -> (l r) p", p=P))
            small(rows[0:64, 1, :], a["norm_g"].rearrange("l i (r p) -> (l i r) p", p=P))
            small(rows[96:112, 0, :], a["s5_lam_re"][0].rearrange("(r g) n -> r (g n)", g=2))
            small(rows[112:128, 0, :], a["s5_lam_im"][0].rearrange("(r g) n -> r (g n)", g=2))
            small(rows[64:68, 1, :], by_p(a["pool_scale"][0]))
            small(rows[68:72, 1, :], by_p(a["s5_d"][0]))
            small(rows[72:88, 1, :], by_p(a["m2_norm_g"][0]))
            small(rows[88:120, 1, :], by_p(a["m2_conv_b"][0]))
            small(rows[:, 2, :], a["m2_conv_w"][0].rearrange("k (r p) -> (k r) p", p=P))
            for i, (kind, n, sl) in enumerate(TILES):
                src, k, w = sources[kind](n)
                if LAST_USER[i] is not None:
                    sp.wait_ge(s["tile_used"], LAST_USER[i] + 1)
                elif sl == 3:
                    sp.wait_ge(s["rows_turned"], 1)
                elif sl in (4, 5):
                    sp.wait_ge(s["q_ready"], 2 * NQ)
                    sp.wait_ge(s["z_ready"], 2 * NQ)
                elif sl == 6:
                    sp.wait_ge(s["bu_mm"], NQ)
                sp.dma_start(slot(sl, k, w), src).then_inc(ring_full[sl], 16)

            wg = a["moe_w_gate"][0].rearrange("e (k p) n -> e p k n", p=P)
            wu = a["moe_w_up"][0].rearrange("e (k p) n -> e p k n", p=P)
            wd = a["moe_w_down"][0].rearrange("e (k p) n -> e p k n", p=P)

            def load_expert(e, k):
                for what, t, m in ORDER:
                    for h in range(m):
                        j = FIRST[what, t] + h
                        sp.wait_ge(s["tile_used"], k * ITEM + (MOE0 + j - RING + 1))
                        if what == "d":
                            dst = slot(j % RING, 4, D)
                            src = wd[bass.ds(e, 1), :, t * 8 + 4 * h:t * 8 + 4 * h + 4, :]
                        else:
                            dst = slot(j % RING, KC, HALF)
                            src = (wg if what == "g" else wu)[bass.ds(e, 1), :, :, (2 * t + h) * HALF:(2 * t + h + 1) * HALF]
                        sp.dma_start(dst, src.rearrange("e p k n -> p (e k) n")).then_inc(ring_full[j % RING], 16)

            with sp.Fori(0, NE) as e:
                load_expert(e, e)
            sp.wait_ge(s["cnt_ready"], 1)
            with sp.register("sp_items") as items:
                sp.reg_mov(items, NE)
                over = sp.value_load(cnt[0:1, 16:17])
                with sp.If(over > 0):
                    with sp.Fori(0, NE) as e:
                        n = sp.value_load(cnt[0:1, bass.ds(e + NE, 1)])
                        with sp.If(n > 0):
                            load_expert(e, sp.snap(items))
                            sp.reg_add(items, items, 1)
            for b in range(NB):
                sp.wait_ge(s["final"], b + 1)
                sp.dma_start(out[0, b * P:(b + 1) * P, :], x[:, b, :]).then_inc(s["stored"], 16)
            sp.wait_ge(s["stored"], 16 * NB)

        @block.gpsimd
        def _(pool):
            c = Counted(pool)
            g = nc.gpsimd
            for dst, v, op, pattern, cm in (
                    (ident[:, :], 0.0, ALU.not_equal, [[-1, P]], 1), (tri[:, :], 1.0, ALU.is_ge, [[1, P]], -1),
                    (ntri[:, :], -1.0, ALU.is_ge, [[1, P]], -1), (after[:, :], 1.0, ALU.is_gt, [[-1, P]], 1),
                    (earlier[:, :, :], 1.0, ALU.is_gt, [[1, NE], [-1, NE]], 0)):
                c.then(g.memset(dst, v), "consts")
                c.inc(g.affine_select(out=dst, in_=dst, compare_op=op, fill=1.0 if op == ALU.not_equal else 0.0,
                                      base=0, pattern=pattern, channel_multiplier=cm), "consts")
                if v == 0.0:
                    c.inc(g.iota(t_row, [[1, TOK]], base=0, channel_multiplier=0,
                                 allow_small_or_imprecise_dtypes=True), "t_iota")
            c.inc(g.memset(ones[:, :], 1.0), "consts")
            c.inc(g.iota(slot_iota[:, :], [[1, P]], base=0, channel_multiplier=0,
                         allow_small_or_imprecise_dtypes=True), "consts")
            for i, win in enumerate(POOL_WINDOWS):
                c.inc(g.memset(inv_cnt[:, i, 16:TOK], 1.0 / win), "inv_tail")
            c.inc(g.memset(ct, 0.0), "ct_zero")
            c.inc(g.memset(bx, 0.0), "bx_zero")
            for i, win in enumerate(POOL_WINDOWS):
                b = band[:, i]
                c.then(g.memset(b, 1.0), "consts")
                c.then(g.affine_select(out=b, in_=b, compare_op=ALU.is_ge, fill=0.0, base=0,
                                       pattern=[[-P, NB], [1, TOK]], channel_multiplier=-1), "consts")
                c.then(g.affine_select(out=b, in_=b, compare_op=ALU.is_ge, fill=0.0, base=win - 1,
                                       pattern=[[P, NB], [-1, TOK]], channel_multiplier=1), "consts")
                pool.wait_ge(s["inv_ready"], 1)
                pool.wait_ge(s["inv_tail"], 4)
                c.then(g.tensor_tensor(b, b, inv_cnt[:, i:i + 1].broadcast_to([P, NB, TOK]), ALU.mult), "band_ready")
            for b in range(NB):
                v = band[:, :, b, b * P:(b + 1) * P]
                c.then(g.tensor_tensor(v, v, ident[:, :].unsqueeze(1).broadcast_to([P, 4, P]), ALU.subtract), "band_ready")
            pool.wait_ge(s["tab_sin"], 2)
            pool.wait_ge(s["pool_out"], 4)
            for q in range(NQ):
                pool.wait_ge(s["z_ready"], 2 * (q + 1))
                if q >= 2:
                    pool.wait_ge(s["y_mm"], q - 1)
                for k in range(2):
                    c.inc(g.tensor_tensor(qq[:, q % 2, k], zz[:, q % 2],
                                          tables[:, 1 - k, q:q + 1, :].broadcast_to([P, 2, TOK]), ALU.mult), "q_ready")
                pool.wait_ge(s["q_ready"], 2 * q + 2)
                c.inc(g.tensor_tensor(qq[:, q % 2, 0, 0], qq[:, q % 2, 0, 0], qq[:, q % 2, 1, 1], ALU.add), "re_ready")
            pool.wait_ge(s["xs_ready"], 8)
            pool.wait_ge(s["da_ready"], 1)
            pool.wait_ge(s["l1_in"], 96)
            for n in range(NB * NG):
                blk, grp = n // NG, n % NG
                if n >= 2:
                    pool.wait_ge(s["y_ready"], n - 1)
                src = xs[:, blk, TOK * grp:TOK * grp + TOK].rearrange("p (j c) -> p j c", j=4)
                for dst, v in ((xdt, hd[:, DT, blk, 4 * grp:4 * grp + 4]),
                               (xd, bro[:, 2 * HEADS + 4 * grp:2 * HEADS + 4 * grp + 4])):
                    c.inc(g.tensor_tensor(dst[:, n % 2].rearrange("p (j c) -> p j c", j=4), src,
                                          v.unsqueeze(2).broadcast_to([P, 4, 64]), ALU.mult), "xdt_ready")

            pool.wait_ge(s["x_ready"], 6)
            g.memset(slots_flat, 0.0).then_inc(s["slots_zero"], 1)
            g.memset(acc, 0.0).then_inc(s["acc_zero"], 1)

            def fetch(n):
                past(pool, "hot_ready", n)
                g.tensor_copy(slots[:, :, :].rearrange("p b i -> p (b i)"),
                              slots_flat[:, bass.ds(n * (3 * NB), 3 * NB)]).then_inc(s["slots_ready"], 1)
            items_loop(pool, "pool", lambda: fetch(0), lambda n: fetch(n + 1), None, False)

        @block.scalar
        def _(act):
            c = Counted(act)
            f = nc.scalar.activation

            def load(dst, src, name):
                act.dma_start(dst, src).then_inc(s[name], 16)

            load(x[:, :, :], a["x"][0].rearrange("(b p) d -> p b d", p=P), "x_in")
            load(log_step, a["s5_log_step"].broadcast_to([P, 2 * NQ]), "s5_in")
            for i, n in enumerate(("s5_b_re", "s5_b_im")):
                load(b_raw[:, i], a[n][0].rearrange("(q g) n h -> (g n) q h", g=2), "s5_in")
            for i, n in enumerate(("s5_c_re", "s5_c_im")):
                for h in range(2):
                    load(c_raw[:, i, :, 64 * h:64 * h + 64], a[n][0].rearrange("(m g) h n -> (g h) m n", m=4), "s5_in")
            load(pw, a["pool_w"][0].rearrange("g p n -> p g n"), "pw_in")
            def ada(i):
                act.wait_ge(s["tile_used"], ADA[i] + 1)
                if i:
                    act.wait_ge(s["ada_turned"], i)
                c.inc(f(modparts[i // NADA], ps[6][:, :], ACT.Copy), "ada_copied")

            def squares(n):
                for b in range(NB):
                    if n:
                        act.wait_ge(s["x_ready"], 2 * n - 1 + b)
                    c.then(f((xn if n else xn0)[:, b], x[:, b], ACT.Square, accum_out=stat[:, b:b + 1]), "sq_done")
                    c.inc(f(stat[:, 2 + b:3 + b], stat[:, b:b + 1], ACT.Sqrt, bias=eps[:, 0:1], scale=1.0 / D), "xroot_done")

            def y_squares(n, base=0, prescale=None):
                f(sqrt_table[:, n - 1:n], eps[:, 0:1], ACT.Sqrt)
                for k, i in enumerate(OUT_ORDER[n - 1]):
                    scale = 1.0 if prescale is None else prescale[:, i // 2:i // 2 + 1]
                    act.wait_ge(s["out_mm"], 4 * (n - 1) + k + 1)
                    c.inc(f(junk_sq[:, i], ps[base + i][:, :], ACT.Square,
                            scale=scale, accum_out=stat[:, 4 + i:5 + i]), "sq_done")
                act.wait_ge(s["root_in"], n)
                c.inc(f(stat[:, 10:12], stat[:, 8:10], ACT.Sqrt, bias=eps[:, 0:1], scale=1.0 / D), "root_done")

            def hT_high(n, n_mod, shift, dst=hT):
                act.wait_ge(s["turned"], n)
                act.wait_ge(s["gs_ready"], n)
                act.wait_ge(s["mod_ready"], n_mod)
                for kc in range(KC // 2, KC):
                    c.inc(f(dst[:, kc], bank(kc // 2, 2, TOK)[:, kc % 2], ACT.Identity, bias=shift[:, kc:kc + 1],
                            scale=gs[:, kc:kc + 1]), "hT_high")

            def grow_rows(n, dst, base=4):
                act.wait_ge(s["grow_mm"], n)
                for h in range(2):
                    c.inc(f(dst[:, HALF * h:HALF * h + HALF], ps[base + h][:, :], ACT.Copy), "grow_ready")

            act.wait_ge(s["cT_zero"], 2)
            act.wait_ge(s["cols_ready"], 1)
            c.inc(f(cT[:, :, 0], cols[:, 1, C_C:C_C + KC], ACT.Silu), "c_ready")
            ada(0)
            act.wait_ge(s["x_in"], 16)
            squares(0)
            ada(1)
            act.wait_ge(s["s5_in"], 112)
            for h in range(2):
                rows_h = slice(64 * h, 64 * h + 64)
                c.inc(f(prm[rows_h, STEP], log_step[rows_h, h:2 * NQ:2], ACT.Exp), "step_exp")
            ada(2)
            act.wait_ge(s["step_ready"], 1)
            c.inc(f(prm[:, MAG], prm[:, LRSTEP], ACT.Exp), "mag_ready")
            ada(3)
            hT_high(1, 4, mod[:, 0, 0])
            act.wait_ge(s["turn_ready"], 1)
            for row in (SIN1, PB):
                c.inc(f(prm[:, row], prm[:, row], ACT.Sin, scale=TWO_PI), "turn_sin")
            act.wait_ge(s["c_turned"], 1)
            act.wait_ge(s["ct_zero"], 1)
            for h in range(2):
                for j in range(4):
                    at = 32 * j + 16 * h
                    for i in range(2):
                        src = bank(4 + i, 4, P)[64 * h:64 * h + 64, :, at:at + 16]
                        dst = ct[64 * h:64 * h + 64, j:NQ:4, i, at:at + 16]
                        c.inc(f(dst, src, ACT.Copy), "ct_ready")
            act.wait_ge(s["tile_used"], AT["mixin", 0] + 1)
            act.wait_ge(s["bx_ready"], 8)
            for b in range(NB):
                c.inc(f(u_tok[:, b], ps[2 + b][:, :], ACT.Copy), "u_ready")
            for i in range(8):
                act.wait_ge(s["b_turned"], i + 1)
                c.inc(f(bt[:, 2 * i:2 * i + 2], bank(6 + i % 2, 2, 2, P), ACT.Copy), "bt_ready")
            act.wait_ge(s["tab_ready"], 1)
            for k in range(2):
                c.inc(f(tables[:, k], tables[:, k], ACT.Sin, scale=TWO_PI), "tab_sin")
            act.wait_ge(s["tile_used"], AT["mixin", 1] + 1)
            act.wait_ge(s["band_ready"], 6)
            for h in range(2):
                c.inc(f(uT[:, 2 * h:2 * h + 2], bank(h, 2, TOK), ACT.Copy), "u_ready")
            load(dtw[:, :, :], w_cols(a["m2_w_in"][0], INNER + 4096, HEADS), "l1_in")
            load(rw[:, :, :], w_cols(a["moe_w_router"][0], 0, NE), "l1_in")
            at = 0
            for n, w in (("m2_dt_bias", HEADS), ("m2_a_log", HEADS), ("m2_d", HEADS), ("moe_b_router", NE)):
                load(bro[:, at:at + w], a[n].broadcast_to([P, w]), "l1_in")
                at += w
            for i in range(4):
                act.wait_ge(s["pool_mm"], i + 1)
                c.inc(f(pool_in[:, i % 2], ps[i % 2][:, 0:TOK], ACT.Copy), "pool_in_ready")
                act.wait_ge(s["pool_out_mm"], i + 1)
                c.inc(f(yT[:, i], ps[i % 2][:, TOK:HALF], ACT.Copy,
                        scale=cols[:, 1, C_PSCALE + i:C_PSCALE + i + 1]), "pool_out")

            def gelu(m):
                act.wait_ge(s["yskip"], m + 1)
                c.inc(f(ys[:, m], ys[:, m], ACT.Gelu_apprx_tanh), "ys_ready")
            for q in range(NQ):
                if q % 2:
                    ada(4 + q // 2)
                if q in (6, 10, 14):
                    gelu((q - 6) // 4)
            gelu(3)
            for m in range(4):
                act.wait_ge(s["glu_mm"], m + 1)
                c.inc(f(uT[:, m], ps[m][:, 0:TOK], ACT.Sigmoid), "glu_sig")
            act.wait_ge(s["ada_turned"], NADA)
            grow_rows(1, grow)
            act.wait_ge(s["q_ready"], 2 * NQ)
            y_squares(1)
            ada(NADA)
            squares(1)
            ada(NADA + 1)
            hT_high(2, NADA, mod[:, 0, 3])

            for t in range(6):
                for j in range(2 if t == 5 else 4):
                    n = 4 * t + j
                    act.wait_ge(s["f_mm"], 2 * n + 1)
                    if n >= 2:
                        act.wait_ge(s["f_act"], n - 1)
                    c.inc(f(silu_f[:, n % 2], ps[4][:, 0:TOK], ACT.Silu), "f_silu")
                if t < 4:
                    ada(NADA + 2 * t + 2)
                    ada(NADA + 2 * t + 3)
            grow_rows(2, grow)
            y_squares(2)
            ada(2 * NADA - 2)

            squares(2)
            ada(2 * NADA - 1)
            hT_high(3, NADA + 10, mod[:, 1, 0])
            act.wait_ge(s["l1_in"], 96)
            c.inc(f(hd[:, TMP1, 0], bro[:, HEADS:2 * HEADS], ACT.Exp), "a_exp")
            act.wait_ge(s["dt_pre"], 1)
            c.then(f(hd[:, TMP0], hd[:, TMP0], ACT.Exp), "dt_exp")
            c.inc(f(hd[:, TMP0], hd[:, TMP0], ACT.Ln, bias=1.0), "dt_ln")

            def xs_copy(m):
                act.wait_ge(s["xs_turned"], 2 * m + 2)
                c.inc(f(xs[:, :, 2 * P * m:2 * P * (m + 1)], bank(4 + m % 2, NB, 2 * P), ACT.Copy), "xs_ready")
            for n in range(32):
                act.wait_ge(s["conv_done"], n + 1)
                if n < 16:
                    if n >= 2:
                        act.wait_ge(s["xs_turned"], n - 1)
                    dst = xsT[:, n % 2]
                else:
                    if n == 16:
                        act.wait_ge(s["tile_used"], LAST_SLOT6 + 1)
                    dst = bc[:, n // 8 - 2, n % 8]
                c.inc(f(dst, conv[:, n % 2], ACT.Silu), "silu_done")
                if n == 4:
                    act.wait_ge(s["cs_mm"], 1)
                    c.inc(f(hd[:, ECS:TOEND + 1], ps[6][:, P:2 * P].rearrange("p (k b h) -> p k b h", k=2, b=NB), ACT.Exp), "cs_exp")
                if n % 2 and 3 <= n <= 17:
                    xs_copy((n - 3) // 2)
                if n in (21, 25):
                    h = (n - 21) // 4
                    act.wait_ge(s["b_turned1"], 4 * h + 4)
                    c.inc(f(btok[:, 4 * h:4 * h + 4], bank(4 + h, 4, P), ACT.Copy), "btok_ready")
            for n in range(NB * NG):
                act.wait_ge(s["dec_min"], n + 1)
                c.inc(f(dmin[:, n % 2], dmin[:, n % 2], ACT.Exp), "dec_exp")
                if n % 2:
                    zi = n // 2
                    act.wait_ge(s["z_mm"], zi + 1)
                    b, sl = zi // 4, zi % 4
                    c.inc(f(zs[:, b, HALF * sl:HALF * sl + HALF], ps[6 + zi % 2][:, :], ACT.Silu), "z_silu")
                if 1 <= n <= NG:
                    act.wait_ge(s["st_mm"], n)
                    c.inc(f(st[:, n - 1], ps[4][:, TOK * ((n - 1) % 2):TOK * ((n - 1) % 2) + TOK], ACT.Copy), "st_ready")
            act.wait_ge(s["y_ready"], NB * NG)
            for m in range(1, 8, 2):
                act.wait_ge(s["y_turned"], m + 1)
                for n in (2 * m, 2 * m + 1):
                    c.inc(f(yT1[:, n], bank(m % 4, 2, TOK)[:, n % 2], ACT.Copy,
                            scale=cols[:, 1, C_M2G + n:C_M2G + n + 1]), "yT1_b")
            for b in range(NB):
                c.then(f(junk_y, zs[:, b], ACT.Square, accum_out=stat[:, 12 + b:13 + b]), "sq_done")
            c.inc(f(stat[:, 14:16], stat[:, 12:14], ACT.Sqrt, bias=eps[:, 0:1], scale=1.0 / INNER), "root_done")
            grow_rows(3, grow1, 0)
            act.wait_ge(s["rg_ready"], 1)
            y_squares(3, 4, rst[:, 4:6])

            squares(3)
            hT_high(4, 2 * NADA, mod[:, 1, 3], hT2)
            act.wait_ge(s["rt_pre"], 1)
            c.inc(f(rt[:, EXPS], rt[:, EXPS], ACT.Exp), "rt_exp")
            grow_rows(4, grow2, 6)

            def item(g, k, nb, m):
                def to_hidden(t):
                    past(act, "e_turned", k * 4 + t + 1)
                    for b, w in enumerate(bank_columns(nb, m, WIDTHS[t])):
                        ins = f(actT[:, t % 2, b, 0:w // P], bank(6 + b, w // P, P), ACT.Copy)
                    ins.then_inc(s["actT_ready"], 1)
                for t in range(4):
                    act.wait_ge(s["tile_used"], k * ITEM + (MOE0 + DONE["g", t]))
                    past(act, "e_turned", k * 4 + t)
                    for b, w in enumerate(bank_columns(nb, m, WIDTHS[t])):
                        ins = f(sg[:, b, 0:w], ps[b][:, 0:w], ACT.Silu)
                    ins.then_inc(s["e_silu"], 1)
                    if t:
                        to_hidden(t - 1)
                to_hidden(3)
                act.wait_ge(s["tile_used"], k * ITEM + (MOE0 + ITEM))
                for dst, src in output_parts(nb, m, 0):
                    ins = f(dst, src, ACT.Copy)
                ins.then_inc(s["y_low"], 1)
            items = items_loop(act, "act", lambda: None, item, None)
            f(sqrt_table[:, 3:4], eps[:, 0:1], ACT.Sqrt)
            past(act, "acc_done", act.snap(items) * 4)
            for b in range(NB):
                c.inc(f(junk_acc[:, b], acc[:, b], ACT.Square, accum_out=stat[:, 8 + b:9 + b]), "sq_done")
            act.wait_ge(s["sq_done"], c.n["sq_done"])
            f(stat[:, 10:12], stat[:, 8:10], ACT.Sqrt, bias=eps[:, 0:1], scale=1.0 / D).then_inc(s["last_root"], 1)

        @block.vector
        def _(dve):
            c = Counted(dve)
            v = nc.vector
            tt, ts, stt = v.tensor_tensor, v.tensor_scalar, v.scalar_tensor_tensor
            step = "dve_step"

            def root(n):
                dve.wait_ge(s["root_done"], n)

            def mods(i):
                dve.wait_ge(s["ada_turned"], i + 1)
                m = modraw[:, i % 2]
                c.then(v.tensor_reduce(m, bank(7, 4, 4, 32)[:, :, :, 0], AX.X, ALU.add), step)
                layer, n = i // NADA, i % NADA
                at = layer * 48 + 4 * n
                c.inc(tt(mod_flat[:, at:at + 4], m, cols[:, 0, at:at + 4], ALU.add), "mod_ready")

            def norm_x(n):
                for b in range(NB):
                    dve.wait_ge(s["xroot_done"], 2 * (n - 1) + b + 1)
                    c.then(v.reciprocal(rst[:, b:b + 1], stat[:, 2 + b:3 + b]), step)
                    c.inc(ts((xn if n > 1 else xn0)[:, b], x[:, b], rst[:, b:b + 1], None, ALU.mult), "xn_ready")

            def scale_cols(n, n_mod, scale, g):
                dve.wait_ge(s["mod_ready"], n_mod)
                if n > 1:
                    dve.wait_ge(s["hT_high"], 4 * (n - 1))
                c.then(stt(gs[:, :], scale, 1.0, g, ALU.add, ALU.mult), "gs_ready")

            def hT_low(n, shift, dst=hT):
                dve.wait_ge(s["turned"], n)
                for kc in range(KC // 2):
                    c.inc(ts(dst[:, kc], bank(kc // 2, 2, TOK)[:, kc % 2], gs[:, kc:kc + 1], shift[:, kc:kc + 1],
                             ALU.mult, ALU.add), "hT_low")

            def gate_cols(n, gate, g):
                dve.wait_ge(s["mod_ready"], c.n["mod_ready"])
                if n > 1:
                    dve.wait_ge(s["grow_mm"], n - 1)
                c.inc(tt(gg[:, :], gate, g, ALU.mult), "gg_ready")

            def residual(n, n_sq, n_root, rows_, base=0, prescaled=False):
                dve.wait_ge(s["grow_ready"], 2 * n)
                for k, i in enumerate(OUT_ORDER[n - 1]):
                    dve.wait_ge(s["sq_done"], n_sq - 3 + k)
                    if k == 3:
                        c.inc(tt(stat[:, 8:10], stat[:, 4:8:2], stat[:, 5:8:2], ALU.add), "root_in")
                    at = slice(HALF * (i % 2), HALF * (i % 2) + HALF)
                    c.inc(tt(tmp[:, i // 2, at], ps[base + i][:, :], rows_[:, at], ALU.mult), step)
                n_tmp = c.n[step]
                root(n_root)
                c.then(v.reciprocal(rst[:, 2:4], stat[:, 10:12]), step)
                if prescaled:
                    c.then(tt(rst[:, 2:4], rst[:, 2:4], rst[:, 4:6], ALU.mult), step)
                dve.wait_ge(s[step], n_tmp)
                for b in range(NB):
                    c.inc(stt(x[:, b], tmp[:, b], rst[:, 2 + b:3 + b], x[:, b], ALU.mult, ALU.add), "x_ready")
                dve.wait_ge(s["x_ready"], 2 * n)

            c.inc(v.memset(cT[:, :, :], 0.0), "cT_zero")
            c.inc(v.memset(eps[:, :], EPS), "cT_zero")
            dve.wait_ge(s["rows_turned"], 1)
            c.then(v.tensor_copy(cols[:, :, :], bank(0, 3, P)), "cols_ready")
            c.then(ts(prm[:, LR], lam_re, -1e-4, None, ALU.min), step)
            dve.wait_ge(s["t_iota"], 1)
            for i, win in enumerate(POOL_WINDOWS):
                c.inc(ts(inv_cnt[:, i, 0:16], t_row[:, 0:16], 1.0, float(win), ALU.add, ALU.min), step)
            dve.wait_ge(s[step], c.n[step])
            c.inc(v.reciprocal(inv_cnt[:, :, 0:16], inv_cnt[:, :, 0:16]), "inv_ready")
            mods(0)
            norm_x(1)
            mods(1)
            dve.wait_ge(s["s5_in"], 112)
            dve.wait_ge(s["step_exp"], 2)
            c.inc(tt(prm[:, LRSTEP], prm[:, LR], prm[:, STEP], ALU.mult), "step_ready")
            c.then(tt(prm[:, TAU], lam_im, prm[:, STEP], ALU.mult), step)
            c.then(ts(prm[:, TAU], prm[:, TAU], INV_TWO_PI, None, ALU.mult), step)
            c.then(ts(prm[:, PA], prm[:, TAU], ROUND, -ROUND, ALU.add, ALU.add), step)
            c.then(tt(prm[:, TAU], prm[:, TAU], prm[:, PA], ALU.subtract), step)
            c.inc(v.tensor_copy(prm[:, SIN1], prm[:, TAU]), step)
            c.then(ts(prm[:, PB], prm[:, TAU], 0.25, None, ALU.is_gt), step)
            c.inc(stt(prm[:, PB], prm[:, TAU], 0.25, prm[:, PB], ALU.add, ALU.subtract), "turn_ready")
            mods(2)
            mods(3)
            scale_cols(1, 4, mod[:, 0, 1], norm_col(0, 0))
            hT_low(1, mod[:, 0, 0])
            dve.wait_ge(s["turn_sin"], 2)
            dve.wait_ge(s["mag_ready"], 1)
            c.then(tt(prm[:, PA], prm[:, MAG], prm[:, PB], ALU.mult), step)
            c.then(tt(prm[:, PB], prm[:, MAG], prm[:, SIN1], ALU.mult), step)
            c.then(ts(prm[:, PA], prm[:, PA], -1.0, None, ALU.add), step)
            c.then(tt(prm[:, PC], prm[:, LR], prm[:, LR], ALU.mult), step)
            c.then(tt(prm[:, INV], lam_im, lam_im, ALU.mult), step)
            c.then(tt(prm[:, INV], prm[:, INV], prm[:, PC], ALU.add), step)
            c.then(v.reciprocal(prm[:, INV], prm[:, INV]), step)
            for dst, p1, p2, op in ((FR, PA, PB, ALU.add), (FI, PB, PA, ALU.subtract)):
                c.then(tt(prm[:, dst], prm[:, p1], prm[:, LR], ALU.mult), step)
                c.then(tt(prm[:, PC], prm[:, p2], lam_im, ALU.mult), step)
                c.then(tt(prm[:, dst], prm[:, dst], prm[:, PC], op), step)
                c.then(tt(prm[:, dst], prm[:, dst], prm[:, INV], ALU.mult), step)
            fr = prm[:, FR].unsqueeze(2).broadcast_to([P, NQ, 16])
            fi = prm[:, FI].unsqueeze(2).broadcast_to([P, NQ, 16])
            for dst, other, op in ((0, 1, ALU.subtract), (1, 0, ALU.add)):
                c.then(tt(bb[:, dst], b_raw[:, dst], fr, ALU.mult), step)
                w = tables[:, 0, :, 0:16]
                c.then(tt(w, b_raw[:, other], fi, ALU.mult), step)
                c.then(tt(bb[:, dst], bb[:, dst], w, op), step)
            dve.wait_ge(s["bx_zero"], 1)
            for h in range(2):
                for j in range(4):
                    at = 32 * j + 16 * h
                    c.inc(v.tensor_copy(bx[64 * h:64 * h + 64, :, j:NQ:4, at:at + 16],
                                        bb[64 * h:64 * h + 64, :, j:NQ:4, :]), "bx_ready")
            tS, tC = tables[:, 0], tables[:, 1]
            c.then(tt(tS, t_row.unsqueeze(1).broadcast_to([P, NQ, TOK]),
                      prm[:, TAU].unsqueeze(2).broadcast_to([P, NQ, TOK]), ALU.mult), step)
            c.then(ts(tC, tS, ROUND, -ROUND, ALU.add, ALU.add), step)
            c.then(tt(tS, tS, tC, ALU.subtract), step)
            c.then(ts(tC, tS, 0.25, None, ALU.is_gt), step)
            c.inc(stt(tC, tS, 0.25, tC, ALU.add, ALU.subtract), "tab_ready")

            def skip(m):
                dve.wait_ge(s["y_mm"], 4 * m + 4)
                c.inc(stt(ys[:, m], uT[:, m], cols[:, 1, C_S5D + m:C_S5D + m + 1], ps[4 + m % 2][:, 0:TOK],
                          ALU.mult, ALU.add), "yskip")
            def states(q):
                dve.wait_ge(s["q_ready"], 2 * q + 2)
                c.inc(tt(qq[:, q % 2, 0, 1], qq[:, q % 2, 0, 1], qq[:, q % 2, 1, 0], ALU.subtract), "im_ready")
            dve.wait_ge(s["u_ready"], 4)
            dve.wait_ge(s["b_turned"], 8)
            dve.wait_ge(s["tab_sin"], 2)
            for q in range(NQ):
                t = temps[:, q % 2]
                dve.wait_ge(s["bu_mm"], q + 1)
                for k in range(2):
                    ins = tt(t[:, k], bank(2 + q % 2, 2, TOK), tables[:, 1 - k, q:q + 1, :].broadcast_to([P, 2, TOK]),
                             ALU.mult)
                    c.then(ins, "bu_used")
                c.inc(tt(t[:, 0, 0], t[:, 0, 0], t[:, 1, 1], ALU.add), step)
                c.then(tt(t[:, 1, 0], t[:, 1, 0], t[:, 0, 1], ALU.subtract), step)
                if q >= 2:
                    dve.wait_ge(s["q_ready"], 2 * (q - 1))
                for k in range(2):
                    c.inc(v.tensor_tensor_scan(zz[:, q % 2, k], prm[:, MAG, q:q + 1].broadcast_to([P, TOK]), t[:, k, 0],
                                               0.0, ALU.mult, ALU.add), "z_ready")
                if q:
                    states(q - 1)
                if q % 2 == 0 and q >= 2:
                    mods(4 + q // 2 - 1)
                if q in (6, 10, 14):
                    skip((q - 6) // 4)
                dve.wait_ge(s["z_ready"], 2 * (q + 1))
            states(NQ - 1)
            mods(NADA - 1)
            skip(3)
            gate_cols(1, mod[:, 0, 2], norm_col(0, 1))
            for m in range(4):
                dve.wait_ge(s["glu_sig"], m + 1)
                c.inc(tt(yT[:, 4 + m], ys[:, m], uT[:, m], ALU.mult), "yT_ready")
            residual(1, 6, 1, grow)
            norm_x(2)
            mods(NADA)
            scale_cols(2, NADA, mod[:, 0, 4], norm_col(0, 2))
            hT_low(2, mod[:, 0, 3])
            gate_cols(2, mod[:, 0, 5], norm_col(0, 3))

            for t in range(6):
                for j in range(2 if t == 5 else 4):
                    n = 4 * t + j
                    if j == 0 and t >= 2:
                        dve.wait_ge(s["tile_used"], AT["down", t - 2] + 1)
                    dve.wait_ge(s["f_mm"], 2 * n + 2)
                    dve.wait_ge(s["f_silu"], n + 1)
                    c.inc(tt(act_f[:, t % 2, j], silu_f[:, n % 2], ps[5][:, 0:TOK], ALU.mult), "f_act")
                if t < 5:
                    mods(NADA + 2 * t + 1)
                if t < 4:
                    mods(NADA + 2 * t + 2)
            residual(2, 12, 2, grow)

            norm_x(3)
            mods(2 * NADA - 2)
            scale_cols(3, NADA + 10, mod[:, 1, 1], norm_col(1, 0))
            hT_low(3, mod[:, 1, 0])
            mods(2 * NADA - 1)
            gate_cols(3, mod[:, 1, 2], norm_col(1, 1))
            dve.wait_ge(s["l1_in"], 96)
            dve.wait_ge(s["dt_mm"], 1)
            dt_bias = bro[:, 0:HEADS].unsqueeze(1).broadcast_to([P, NB, HEADS])
            c.then(tt(hd[:, DA], bank(6, NB, HEADS), dt_bias, ALU.add), step)
            c.inc(stt(hd[:, TMP0], hd[:, DA], -1.0, hd[:, DA], ALU.mult, ALU.min), "dt_pre")
            c.inc(ts(hd[:, DT], hd[:, DA], 0.0, None, ALU.max), step)
            dve.wait_ge(s[step], c.n[step])
            dve.wait_ge(s["dt_ln"], 1)
            dve.wait_ge(s["a_exp"], 1)
            c.then(tt(hd[:, DT], hd[:, DT], hd[:, TMP0], ALU.add), step)
            c.then(stt(hd[:, DA], hd[:, DT], -1.0, hd[:, TMP1, 0:1].broadcast_to([P, NB, HEADS]), ALU.mult, ALU.mult),
                   "da_ready")
            for n in range(32):
                dve.wait_ge(s["xbc_mm"], n + 1)
                if n >= 2:
                    dve.wait_ge(s["silu_done"], n - 1)
                y, p = conv[:, n % 2], ps[n % 4]

                def tap(k):
                    return cols[:, 2, 32 * k + n:32 * k + n + 1]
                c.then(ts(y, p[:, 0:TOK], tap(3), cols[:, 1, C_CONVB + n:C_CONVB + n + 1], ALU.mult, ALU.add), step)
                for k in (2, 1):
                    c.then(stt(y[:, 3 - k:TOK], p[:, 0:TOK - 3 + k], tap(k), y[:, 3 - k:TOK], ALU.mult, ALU.add), step)
                c.inc(stt(y[:, 3:TOK], p[:, 0:TOK - 3], tap(0), y[:, 3:TOK], ALU.mult, ALU.add), "conv_done")

            def mixed(n):
                blk, grp = n // NG, n % NG
                dve.wait_ge(s["dec_exp"], n + 1)
                if n >= 2:
                    dve.wait_ge(s["y1_mm"], n - 1)
                c.inc(tt(mix[:, n % 2].rearrange("p (j l) -> p j l", j=4), dmin[:, n % 2].rearrange("p (j l) -> p j l", j=4),
                         cbm[:, n % 2:n % 2 + 1].broadcast_to([P, 4, P]), ALU.mult), "m_ready")
                if blk == 0:
                    dve.wait_ge(s["xdt_ready"], 2 * n + 1)
                    if n >= 2:
                        dve.wait_ge(s["st_mm"], n - 1)
                    c.inc(tt(xw[:, n % 2].rearrange("p (j c) -> p j c", j=4),
                             xdt[:, n % 2].rearrange("p (j c) -> p j c", j=4),
                             hd[:, TOEND, 0, 4 * grp:4 * grp + 4].unsqueeze(2).broadcast_to([P, 4, 64]), ALU.mult), "xw_ready")

            def gated(n):
                blk, grp = n // NG, n % NG
                bk = ps[3 + 2 * (n % 2)]
                o = yo[:, n % 2]
                dve.wait_ge(s["y1_mm"], n + 1)
                dve.wait_ge(s["xdt_ready"], 2 * n + 2)
                if blk:
                    c.then(tt(o.rearrange("p (j c) -> p j c", j=4), bk[:, TOK:HALF].rearrange("p (j c) -> p j c", j=4),
                              hd[:, ECS, 1, 4 * grp:4 * grp + 4].unsqueeze(2).broadcast_to([P, 4, 64]), ALU.mult), step)
                    c.then(tt(o, o, xd[:, n % 2], ALU.add), step)
                    c.then(tt(o, o, bk[:, 0:TOK], ALU.add), step)
                else:
                    c.then(tt(o, bk[:, 0:TOK], xd[:, n % 2], ALU.add), step)
                dve.wait_ge(s["z_silu"], 4 * blk + grp // 2 + 1)
                z = zs[:, blk, TOK * grp:TOK * grp + TOK]
                c.inc(tt(z, o, z, ALU.mult), "y_ready")
            dve.wait_ge(s["cs_exp"], 1)
            for n in range(NB * NG):
                dve.wait_ge(s["cb_mm"], n + 1)
                if n >= 2:
                    dve.wait_ge(s["m_ready"], n - 1)
                c.inc(tt(cbm[:, n % 2], ps[2][:, P * (n % 2):P * (n % 2) + P], tri[:, :], ALU.mult), "cbm_ready")
                dve.wait_ge(s["dec_mm"], n + 1)
                c.inc(ts(dmin[:, n % 2], ps[n % 2][:, :], 0.0, None, ALU.min), "dec_min")
                dve.wait_ge(s["cbm_ready"], n + 1)
                if n >= 1:
                    mixed(n - 1)
                if n >= 2:
                    gated(n - 2)
            mixed(NB * NG - 1)
            gated(NB * NG - 2)
            gated(NB * NG - 1)
            for m in range(0, 8, 2):
                dve.wait_ge(s["y_turned"], m + 1)
                for n in (2 * m, 2 * m + 1):
                    c.inc(ts(yT1[:, n], bank(m % 4, 2, TOK)[:, n % 2], cols[:, 1, C_M2G + n:C_M2G + n + 1], None, ALU.mult),
                          "yT1_a")
            root(3)
            c.inc(v.reciprocal(rst[:, 4:6], stat[:, 14:16]), "rg_ready")
            dve.wait_ge(s["rg_ready"], 1)
            residual(3, 20, 4, grow1, 4, True)

            scale_cols(4, 2 * NADA, mod[:, 1, 4], norm_col(1, 2))
            norm_x(4)
            gate_cols(4, mod[:, 1, 5], norm_col(1, 3))
            hT_low(4, mod[:, 1, 3], hT2)
            dve.wait_ge(s["logit_mm"], 1)
            r_bias = bro[:, 3 * HEADS:3 * HEADS + NE].unsqueeze(1).broadcast_to([P, NB, NE])
            c.then(tt(rt[:, LOGIT], bank(4, NB, NE), r_bias, ALU.add), step)
            c.then(v.tensor_reduce(rst[:, 6:8], rt[:, LOGIT], AX.X, ALU.max), step)
            c.inc(tt(rt[:, EXPS], rt[:, LOGIT], rst[:, 6:8].unsqueeze(2).broadcast_to([P, NB, NE]), ALU.subtract), "rt_pre")
            other = rt[:, LOGIT].unsqueeze(2).broadcast_to([P, NB, NE, NE])
            own = rt[:, LOGIT].unsqueeze(3).broadcast_to([P, NB, NE, NE])
            gt_, eq_ = pair[:, 0], pair[:, 1]
            c.inc(tt(gt_, other, own, ALU.is_gt), step)
            c.then(tt(eq_, other, own, ALU.is_equal), step)
            c.then(tt(eq_, eq_, earlier[:, :, :].unsqueeze(1).broadcast_to([P, NB, NE, NE]), ALU.mult), step)
            c.then(tt(gt_, gt_, eq_, ALU.add), step)
            c.then(v.tensor_reduce(rt[:, RANK], gt_, AX.X, ALU.add), step)
            c.then(ts(rt[:, SEL], rt[:, RANK], 2.0, None, ALU.is_lt), "mask_ready")
            dve.wait_ge(s["rt_exp"], 1)
            c.then(tt(rt[:, GATE], rt[:, EXPS], rt[:, SEL], ALU.mult), step)
            c.then(v.tensor_reduce(rst[:, 8:10], rt[:, GATE], AX.X, ALU.add), step)
            c.then(v.reciprocal(rst[:, 8:10], rst[:, 8:10]), step)
            c.then(tt(rt[:, GATE], rt[:, GATE], rst[:, 8:10].unsqueeze(2).broadcast_to([P, NB, NE]), ALU.mult), step)
            dve.wait_ge(s["pos_mm"], 1)
            c.then(stt(rt[:, POS], bank(1, NB, NE), 999.0, rt[:, SEL], ALU.add, ALU.mult), step)
            dve.wait_ge(s["slots_zero"], 1)
            for p in range(2):
                by_expert = slots_of[:, p].rearrange("p e b i -> p i b e")
                c.inc(ts(by_expert[:, 0], rt[:, POS], -1000.0 - P * p, None, ALU.add), step)
                c.inc(v.tensor_copy(by_expert[:, 1], rt[:, GATE]), step)
                c.inc(v.tensor_copy(by_expert[:, 2], rst[:, 0:2].unsqueeze(2).broadcast_to([P, NB, NE])), step)
            total = ps[1][0:1, 2 * NE:3 * NE]
            c.inc(ts(cnt_f[:, 0:NE], total, 1.0, None, ALU.max), step)
            c.then(ts(cnt_f[:, NE:2 * NE], total, -float(P), None, ALU.add), step)
            c.then(v.tensor_reduce(cnt_f[:, 16:17], cnt_f[:, NE:2 * NE], AX.X, ALU.max), step)
            c.inc(v.tensor_copy(cnt[:, :], cnt_f[:, :]), "cnt_ready")
            dve.wait_ge(s["cnt_ready"], 1)

            def build_hot(n):
                past(dve, "slots_ready", n + 1)
                past(dve, "gather_mm", n * 2)
                past(dve, "gT_mm", n)
                for b in range(NB):
                    pos, gate, rms = (slots[:, b, i:i + 1] for i in range(3))
                    ts(hot[:, b], slot_iota[:, :], pos, rms, ALU.is_equal, ALU.mult)
                    ins = ts(hotg[:, b], slot_iota[:, :], pos, gate, ALU.is_equal, ALU.mult)
                ins.then_inc(s["hot_ready"], 1)

            def take_tokens(n, used):
                dve.wait_ge(s["tile_used"], used)
                for kc in range(KC):
                    if kc % 4 == 0:
                        past(dve, "gather_mm", n * 2 + kc // 4 + 1)
                    ins = ts(hcur3[:, kc], bank(kc // 4, 4, P)[:, kc % 4], gs[:, kc:kc + 1], mod[:, 1, 3, kc:kc + 1],
                             ALU.mult, ALU.add)
                ins.then_inc(s["hg_ready"], 1)

            def take_gates(n, k):
                past(dve, "gT_mm", n + 1)
                past(dve, "scat_mm", k * 4)
                v.tensor_copy(gcur, ps[3][:, 0:TOK]).then_inc(s["gT_ready"], 1)

            def gather(n, k):
                build_hot(n)
                take_tokens(n, k * ITEM + MOE0)
                take_gates(n, k)

            def item(g, k, nb, m):
                for t in range(4):
                    dve.wait_ge(s["tile_used"], k * ITEM + (MOE0 + DONE["u", t]))
                    past(dve, "e_silu", k * 4 + t + 1)
                    for b, w in enumerate(bank_columns(nb, m, WIDTHS[t])):
                        ins = tt(sg[:, b, 0:w], sg[:, b, 0:w], ps[2 + b][:, 0:w], ALU.mult)
                    ins.then_inc(s["e_act"], 1)
                    if t == 0:
                        build_hot(g + 1)
                take_tokens(g + 1, k * ITEM + (MOE0 + DONE["u", 3]))
                dve.wait_ge(s["tile_used"], k * ITEM + (MOE0 + ITEM))
                for dst, src in output_parts(nb, m, 1):
                    ins = v.tensor_copy(dst, src)
                ins.then_inc(s["y_high"], 1)
                past(dve, "acc_done", k * 4)
                for i in range(4):
                    o = acc[:, i // 2, HALF * (i % 2):HALF * (i % 2) + HALF]
                    past(dve, "scat_mm", k * 4 + i + 1)
                    tt(o, o, ps[SCATTER[i]][:, :], ALU.add).then_inc(s["acc_done"], 1)
                take_gates(g + 1, k + 1)
            dve.wait_ge(s["acc_zero"], 1)
            items = items_loop(dve, "dve", lambda: gather(0, 0), item, lambda g, k: gather(g + 1, k))
            past(dve, "acc_done", dve.snap(items) * 4)
            dve.wait_ge(s["grow_ready"], 8)
            for b in range(NB):
                c.inc(tt(tmp2[:, b], acc[:, b], grow2, ALU.mult), "last_scaled")
            dve.wait_ge(s["last_root"], 1)
            c.then(v.reciprocal(rst[:, 2:4], stat[:, 10:12]), step)
            dve.wait_ge(s["last_scaled"], 2)
            for b in range(NB):
                c.inc(stt(x[:, b], tmp2[:, b], rst[:, 2 + b:3 + b], x[:, b], ALU.mult, ALU.add), "final")

        @block.tensor
        def _(pe):
            mm, turn = nc.tensor.matmul, nc.tensor.transpose

            def arrived(i):
                pe.wait_ge(ring_full[TILES[i][2]], 16 * FILL[i])
                return TILES[i][2]

            def chain(out_, pairs, **kw):
                for i, (l, r) in enumerate(pairs):
                    ins = mm(out_, l, r, start=i == 0, stop=i == len(pairs) - 1, **kw)
                return ins

            def stay_warm(n, bk):
                for _ in range(n):
                    mm(ps[bk][:, 0:P], ident[:, :], ident[:, :], start=True, stop=True)

            def first_chain(out_, pairs, n):
                for i, kc in enumerate((0, 4, 1, 5, 2, 6, 3, 7)):
                    pe.wait_ge(s["hT_high" if kc >= 4 else "hT_low"], 4 * (n - 1) + kc % 4 + 1)
                    l, r = pairs[kc]
                    ins = mm(out_, l, r, start=i == 0, stop=i == KC - 1)
                return ins

            def ada_mm(i):
                if i:
                    pe.wait_ge(s["ada_copied"], i)
                w = slot(arrived(ADA[i]), KC, HALF)
                for half in range(2):
                    for j in range(4):
                        kc = 2 * j + half
                        ins = mm(ps[6][32 * j:32 * j + 32, :], cT[:, kc, :], w[:, kc, :], start=half == 0, stop=half == 1)
                ins.then_inc(s["tile_used"], 1)

            def ada_turn(i):
                pe.wait_ge(s["ada_copied"], i + 1)
                if i:
                    pe.wait_ge(s["mod_ready"], i)
                for k in range(4):
                    ins = turn(ps[7][:, P * k:P * k + P], modparts[i // NADA][:, P * k:P * k + P], ident[:, :])
                ins.then_inc(s["ada_turned"], 1)

            def turn_x(n):
                for b in range(NB):
                    pe.wait_ge(s["xn_ready"], 2 * (n - 1) + b + 1)
                    for kc in range(KC):
                        ins = turn(ps[kc // 2][:, TOK * (kc % 2) + P * b:TOK * (kc % 2) + P * b + P],
                                   (xn if n > 1 else xn0)[:, b, P * kc:P * kc + P], ident[:, :])
                ins.then_inc(s["turned"], 1)

            def row_products(col, base):
                for kc in range(KC):
                    ins = mm(ps[base + kc // 4][:, P * (kc % 4):P * (kc % 4) + P], col[:, kc:kc + 1].broadcast_to([P, P]),
                             ident[:, :], start=True, stop=True)
                return ins

            pe.wait_ge(s["consts"], 2)
            stay_warm(WARM_ROWS, 5)
            pe.wait_ge(s["small_in"], 160)
            for i in range(3):
                ins = turn(ps[0][:, P * i:P * i + P], rows[:, i, :], ident[:, :])
            ins.then_inc(s["rows_turned"], 1)
            stay_warm(WARM_C, 5)
            pe.wait_ge(s["c_ready"], 1)
            for i in range(3):
                ada_mm(i)
                ada_turn(i)
                stay_warm(WARM_ADA, 5)
            ada_mm(3)
            pe.wait_ge(s["cols_ready"], 1)
            turn_x(1)
            ada_turn(3)
            pe.wait_ge(s["s5_in"], 112)
            for i in range(2):
                for m in range(4):
                    ins = turn(ps[4 + i][:, P * m:P * m + P], c_raw[:, i, m], ident[:, :])
            ins.then_inc(s["c_turned"], 1)

            w = slot(arrived(AT["mixin", 0]), KC, HALF)
            for b in range(NB):
                pairs = [(hT[:, kc, P * b:P * b + P], w[:, kc]) for kc in range(KC)]
                if b == 0:
                    pe.wait_ge(s["hT_high"], 2)
                    first_chain(ps[2][:, :], pairs, 1)
                else:
                    ins = chain(ps[3][:, :], pairs)
            ins.then_inc(s["tile_used"], 1)
            pe.wait_ge(s["mod_ready"], 4)
            pe.wait_ge(s["bx_ready"], 8)
            for i in range(8):
                if i >= 2:
                    pe.wait_ge(s["bt_ready"], i - 1)
                for k in range(4):
                    ins = turn(ps[6 + i % 2][:, P * k:P * k + P], bx[:, k % 2, 2 * i + k // 2], ident[:, :])
                ins.then_inc(s["b_turned"], 1)
            w = slot(arrived(AT["mixin", 1]), KC, HALF)
            for m in range(4):
                ins = chain(ps[m // 2][:, TOK * (m % 2):TOK * (m % 2) + TOK],
                            [(w[:, kc, P * m:P * m + P], hT[:, kc]) for kc in range(KC)])
            ins.then_inc(s["tile_used"], 1)
            pe.wait_ge(s["u_ready"], 4)
            pe.wait_ge(s["band_ready"], 6)
            pe.wait_ge(s["pw_in"], 16)
            for i in range(4):
                if i >= 2:
                    pe.wait_ge(s["pool_out"], i - 1)
                chain(ps[i % 2][:, 0:TOK], [(u_tok[:, b, P * i:P * i + P], band[:, i, b]) for b in range(NB)])\
                    .then_inc(s["pool_mm"], 1)
                pe.wait_ge(s["pool_in_ready"], i + 1)
                chain(ps[i % 2][:, TOK:HALF], [(pw[:, i], pool_in[:, i % 2])]).then_inc(s["pool_out_mm"], 1)

            pe.wait_ge(s["bt_ready"], 8)
            pe.wait_ge(s["ct_ready"], 16)

            def s5_out(q):
                pe.wait_ge(s["re_ready"], q + 1)
                pe.wait_ge(s["im_ready"], q + 1)
                m = q // 4
                if q % 4 == 0 and m >= 2:
                    pe.wait_ge(s["yskip"], m - 1)
                z = qq[:, q % 2]
                for i in range(2):
                    ins = mm(ps[4 + m % 2][:, 0:TOK], ct[:, q, i], z[:, 0, i], start=q % 4 == 0 and i == 0,
                             stop=q % 4 == 3 and i == 1)
                ins.then_inc(s["y_mm"], 1)
            def s5_in(q):
                if q >= 2:
                    pe.wait_ge(s["bu_used"], 2 * (q - 1))
                for k in range(2):
                    ins = mm(ps[2 + q % 2][:, TOK * k:TOK * k + TOK], bt[:, q, k], uT[:, q // 4], start=True, stop=True)
                ins.then_inc(s["bu_mm"], 1)
            s5_in(0)
            for q in range(NQ):
                if q + 1 < NQ:
                    s5_in(q + 1)
                if q % 2 == 0 and q >= 2:
                    ada_turn(4 + q // 2 - 1)
                if q >= 2:
                    s5_out(q - 2)
                if q % 2:
                    ada_mm(4 + q // 2)
            ada_turn(NADA - 1)
            s5_out(NQ - 2)
            s5_out(NQ - 1)
            pe.wait_ge(s["ys_ready"], 4)
            pe.wait_ge(s["pool_out"], 4)
            pe.wait_ge(s["bu_used"], 2 * NQ)
            w = slot(arrived(AT["glu", 0]), 4, HALF)
            for m in range(4):
                chain(ps[m][:, 0:TOK], [(w[:, k, P * m:P * m + P], ys[:, k]) for k in range(4)]).then_inc(s["glu_mm"], 1)
            pe.wait_ge(s["gg_ready"], 1)
            pe.wait_ge(s["yskip"], 4)
            row_products(gg, 4).then_inc(s["grow_mm"], 1)
            pe.wait_ge(s["yT_ready"], 4)
            pe.wait_ge(s["glu_sig"], 4)
            pe.wait_ge(s["glu_mm"], 4)
            for h in range(2):
                i = AT["mixout", h]
                w = slot(arrived(i), KC, HALF)
                if h == 0:
                    pe.sem_inc(s["tile_used"], 1)
                for b in range(NB):
                    chain(ps[2 * b + h][:, :], [(yT[:, kc, P * b:P * b + P], w[:, kc]) for kc in range(KC)])\
                        .then_inc(s["out_mm"], 1)
                pe.wait_ge(s["out_mm"], 2 * h + 2)
                pe.sem_inc(s["tile_used"], 1)

            ada_mm(NADA)
            ada_turn(NADA)
            ada_mm(NADA + 1)
            pe.wait_ge(s["x_ready"], 2)
            turn_x(2)
            pe.wait_ge(s["grow_ready"], 2)

            def ffn_down(t):
                n = 2 if t == 5 else 4
                w = slot(arrived(AT["down", t]), n, D)
                pe.wait_ge(s["f_act"], 4 * t + n)
                for i in range(4):
                    b, h = i // 2, i % 2
                    for j in range(n):
                        ins = mm(ps[i][:, :], act_f[:, t % 2, j, P * b:P * b + P], w[:, j, HALF * h:HALF * h + HALF],
                                 start=t == 0 and j == 0, stop=t == 5 and j == n - 1)
                    if t == 5:
                        ins.then_inc(s["out_mm"], 1)
                if t < 5:
                    ins.then_inc(s["tile_used"], 1)
                else:
                    pe.wait_ge(s["out_mm"], 8)
                    pe.sem_inc(s["tile_used"], 1)
            for t in range(6):
                n_f = 2 if t == 5 else 4
                g, u = AT["gate", t], AT["up", t]
                wg = slot(arrived(g), KC, P * n_f)
                wu = slot(arrived(u), KC, P * n_f)
                for j in range(n_f):
                    n = 4 * t + j
                    for k, w in enumerate((wg, wu)):
                        if n:
                            pe.wait_ge(s["f_act" if k else "f_silu"], n)
                        pairs = [(w[:, kc, P * j:P * j + P], hT[:, kc]) for kc in range(KC)]
                        ins = chain(ps[4 + k][:, 0:TOK], pairs) if n or k else first_chain(ps[4][:, 0:TOK], pairs, 2)
                        ins.then_inc(s["f_mm"], 1)
                if t < 5:
                    ada_turn(NADA + 2 * t + 1)
                pe.wait_ge(s["f_mm"], 8 * t + 2 * n_f)
                pe.sem_inc(s["tile_used"], 2)
                if t < 4:
                    ada_mm(NADA + 2 * t + 2)
                if t:
                    ffn_down(t - 1)
                if t < 4:
                    ada_turn(NADA + 2 * t + 2)
                    ada_mm(NADA + 2 * t + 3)
            pe.wait_ge(s["gg_ready"], 2)
            pe.wait_ge(s["f_act"], 22)
            row_products(gg, 4).then_inc(s["grow_mm"], 1)
            ffn_down(5)
            ada_mm(2 * NADA - 2)
            ada_turn(2 * NADA - 2)
            ada_mm(2 * NADA - 1)

            pe.wait_ge(s["x_ready"], 4)
            turn_x(3)
            ada_turn(2 * NADA - 1)

            def turn_conv(n):
                pe.wait_ge(s["silu_done"], n + 1)
                if n < 16:
                    m = n // 2
                    if n % 2 == 0 and m >= 2:
                        pe.wait_ge(s["xs_ready"], m - 1)
                    for b in range(NB):
                        at = TOK * b + P * (n % 2)
                        ins = turn(ps[4 + m % 2][:, at:at + P], xsT[:, n % 2, P * b:P * b + P], ident[:, :])
                    ins.then_inc(s["xs_turned"], 1)
                else:
                    g = n - 16
                    if g % 4 == 0:
                        pe.wait_ge(s["xs_ready"], 7 + g // 4)
                    turn(ps[4 + g // 4][:, P * (g % 4):P * (g % 4) + P], bc[:, 0, g, 0:P], ident[:, :])\
                        .then_inc(s["b_turned1"], 1)
            pe.wait_ge(s["grow_ready"], 4)
            for n in range(32):
                i = AT["xbc", n // 4]
                if n % 4 == 0:
                    w = slot(arrived(i), KC, HALF)
                if n >= 4:
                    pe.wait_ge(s["conv_done"], n - 3)
                pairs = [(w[:, kc, P * (n % 4):P * (n % 4) + P], hT[:, kc]) for kc in range(KC)]
                if n == 0:
                    pe.wait_ge(s["hT_low"], 10)
                ins = chain(ps[n % 4][:, 0:TOK], pairs) if n else first_chain(ps[0][:, 0:TOK], pairs, 3)
                ins.then_inc(s["xbc_mm"], 1)
                if n == 0:
                    pe.wait_ge(s["l1_in"], 96)
                    pe.wait_ge(s["ada_copied"], 2 * NADA)
                    for b in range(NB):
                        ins = chain(ps[6][:, HEADS * b:HEADS * b + HEADS],
                                    [(hT[:, kc, P * b:P * b + P], dtw[:, kc, :]) for kc in range(KC)])
                    ins.then_inc(s["dt_mm"], 1)
                if n % 4 == 3:
                    pe.wait_ge(s["xbc_mm"], n + 1)
                    pe.sem_inc(s["tile_used"], 1)
                if 2 <= n < 26:
                    turn_conv(n - 2)
                if n == 4:
                    pe.wait_ge(s["consts"], 12)
                    pe.wait_ge(s["da_ready"], 1)
                    for k, m in enumerate((tri, after)):
                        for b in range(NB):
                            at = P + 2 * HEADS * k + HEADS * b
                            ins = mm(ps[6][:, at:at + HEADS], m[:, :], hd[:, DA, b], start=True, stop=True)
                    ins.then_inc(s["cs_mm"], 1)

            pe.wait_ge(s["mod_ready"], 2 * NADA)
            def z_part(n):
                zi = n // 2
                b, sl = zi // 4, zi % 4
                if n % 2 == 0:
                    if zi >= 2:
                        pe.wait_ge(s["z_silu"], zi - 1)
                    if zi < 4:
                        arrived(AT["z", sl])
                w = slot(TILES[AT["z", sl]][2], KC, HALF)
                for kc in range(4 * (n % 2), 4 * (n % 2) + 4):
                    ins = mm(ps[6 + zi % 2][:, :], hT[:, kc, P * b:P * b + P], w[:, kc], start=kc == 0, stop=kc == KC - 1)
                if n % 2:
                    ins.then_inc(s["z_mm"], 1)
                    if b == 1:
                        pe.wait_ge(s["z_mm"], zi + 1)
                        pe.sem_inc(s["tile_used"], 1)

            def y_products(n):
                blk, grp = n // NG, n % NG
                bk = ps[3 + 2 * (n % 2)]
                pe.wait_ge(s["m_ready"], n + 1)
                pe.wait_ge(s["xdt_ready"], 2 * n + 1)
                if n >= 2:
                    pe.wait_ge(s["y_ready"], n - 1)
                for j in range(4):
                    ins = mm(bk[:, 64 * j:64 * j + 64], mix[:, n % 2, P * j:P * j + P], xdt[:, n % 2, 64 * j:64 * j + 64],
                             start=True, stop=True)
                if blk:
                    pe.wait_ge(s["st_ready"], grp + 1)
                    ins = mm(bk[:, TOK:HALF], bc[:, 1, grp, P:TOK], st[:, grp], start=True, stop=True)
                ins.then_inc(s["y1_mm"], 1)
                if blk == 0:
                    pe.wait_ge(s["xw_ready"], n + 1)
                    if n:
                        pe.wait_ge(s["st_ready"], n)
                    mm(ps[4][:, TOK * (n % 2):TOK * (n % 2) + TOK], btok[:, grp], xw[:, n % 2], start=True, stop=True)\
                        .then_inc(s["st_mm"], 1)
            pe.wait_ge(s["cs_exp"], 1)
            z_part(0)
            pe.wait_ge(s["conv_done"], 32)
            for n in range(NB * NG):
                blk, grp = n // NG, n % NG
                if n >= 2:
                    pe.wait_ge(s["dec_min"], n - 1)
                da = hd[:, DA, blk, 4 * grp:4 * grp + 4]
                dec = bank(n % 2, 4, P)
                mm(dec, ntri[:, :], da.unsqueeze(2).broadcast_to([P, 4, P]), start=True, stop=False, skip_group_check=True)
                for j in range(4):
                    ins = mm(dec[:, j], da[:, j:j + 1].broadcast_to([P, P]), tri[:, :], start=False, stop=j == 3,
                             skip_group_check=True)
                ins.then_inc(s["dec_mm"], 1)
                if n:
                    pe.wait_ge(s["cbm_ready"], n)
                else:
                    pe.wait_ge(s["silu_done"], 32)
                    pe.wait_ge(s["btok_ready"], 2)
                mm(ps[2][:, P * (n % 2):P * (n % 2) + P], bc[:, 0, grp, P * blk:P * blk + P], bc[:, 1, grp, P * blk:P * blk + P],
                   start=True, stop=True).then_inc(s["cb_mm"], 1)
                if n:
                    z_part(n)
                    y_products(n - 1)
            y_products(NB * NG - 1)
            pe.wait_ge(s["dec_min"], NB * NG)
            pe.wait_ge(s["cbm_ready"], NB * NG)
            for n in range(16):
                m = n // 2
                pe.wait_ge(s["y_ready"], NG + max(m + 1, NG - 1 if m == 3 else 0))
                if n % 2 == 0 and m >= 4:
                    pe.wait_ge(s["yT1_b" if m % 2 else "yT1_a"], 2 * ((m - 4) // 2) + 2)
                for b in range(NB):
                    at = TOK * (n % 2) + P * b
                    ins = turn(ps[m % 4][:, at:at + P], zs[:, b, P * n:P * n + P], ident[:, :])
                if n % 2:
                    ins.then_inc(s["y_turned"], 1)
            pe.wait_ge(s["st_ready"], NG)
            pe.wait_ge(s["z_silu"], 8)
            for t in range(4):
                w = slot(arrived(AT["m2out", t]), 4, D)
                if t == 2:
                    pe.wait_ge(s["yT1_a"], 8)
                    pe.wait_ge(s["yT1_b"], 8)
                    pe.wait_ge(s["gg_ready"], 3)
                    row_products(gg, 0).then_inc(s["grow_mm"], 1)
                for pair_ in ((0, 1), (2, 3)) if t < 3 else ((0, 1, 2, 3),):
                    for j in pair_:
                        pe.wait_ge(s["yT1_b" if j // 2 else "yT1_a"], 2 * t + j % 2 + 1)
                    for i in range(4):
                        b, h = i // 2, i % 2
                        for j in pair_:
                            ins = mm(ps[4 + i][:, :], yT1[:, 4 * t + j, P * b:P * b + P], w[:, j, HALF * h:HALF * h + HALF],
                                     start=t == 0 and j == 0, stop=t == 3 and j == 3)
                        if t == 3:
                            ins.then_inc(s["out_mm"], 1)
                if t < 3:
                    ins.then_inc(s["tile_used"], 1)
                else:
                    pe.wait_ge(s["out_mm"], 12)
                    pe.sem_inc(s["tile_used"], 2)

            pe.wait_ge(s["yT1_a"], 8)
            pe.wait_ge(s["yT1_b"], 8)
            pe.wait_ge(s["grow_ready"], 6)
            stay_warm(WARM_NORM, 0)
            pe.wait_ge(s["x_ready"], 6)
            turn_x(4)
            pe.wait_ge(s["hT_low"], 16)
            pe.wait_ge(s["hT_high"], 16)
            for b in range(NB):
                ins = chain(ps[4][:, NE * b:NE * b + NE], [(hT2[:, kc, P * b:P * b + P], rw[:, kc, :]) for kc in range(KC)])
            ins.then_inc(s["logit_mm"], 1)
            pe.wait_ge(s["gg_ready"], 4)
            row_products(gg, 6).then_inc(s["grow_mm"], 1)
            pe.wait_ge(s["mask_ready"], 1)
            sel = rt[:, SEL]
            chain(ps[1][:, 0:NE], [(tri[:, :], sel[:, 0])])
            chain(ps[1][:, NE:2 * NE], [(tri[:, :], sel[:, 1]), (ones[:, :], sel[:, 0])])
            chain(ps[1][:, 2 * NE:3 * NE], [(ones[:, :], sel[:, 0]), (ones[:, :], sel[:, 1])]).then_inc(s["pos_mm"], 1)

            def gather(n, k):
                past(pe, "hot_ready", n + 1)
                past(pe, "e_silu", k * 4)
                past(pe, "hg_ready", n)
                for kc in range(KC):
                    ins = chain(ps[kc // 4][:, P * (kc % 4):P * (kc % 4) + P],
                                [(x[:, b, P * kc:P * kc + P], hot[:, b]) for b in range(NB)])
                    if kc % 4 == 3:
                        ins.then_inc(s["gather_mm"], 1)
                past(pe, "e_act", k * 4)
                past(pe, "gT_ready", n)
                for b in range(NB):
                    ins = turn(ps[3][:, P * b:P * b + P], hotg[:, b], ident[:, :])
                ins.then_inc(s["gT_mm"], 1)

            def item(g, k, nb, m):
                fill = [k * 48 + 16 * FILLS0[i] for i in range(RING)]
                parts, per = P // m, 64 // m

                def expert_tile(what, t, h):
                    j = FIRST[what, t] + h
                    pe.wait_ge(ring_full[j % RING], fill[j % RING] + 16 * (j // RING + 1))
                    return j % RING

                def hidden(what, t, base):
                    w = WIDTHS[t] // per
                    sl = [slot(expert_tile(what, t, h), KC, HALF) for h in range(2 if t < 3 else 1)]
                    for b in range(nb):
                        for kc in range(KC):
                            for h in range(parts):
                                at = w * h
                                ins = mm(ps[base + b // per][m * h:m * h + m, w * (b % per):w * (b % per) + w],
                                         hcur3[:, kc, m * b:m * b + m], sl[at // HALF][:, kc, at % HALF:at % HALF + w],
                                         start=kc == 0, stop=kc == KC - 1)
                    ins.then_inc(s["tile_used"], 2 if t < 3 else 1)

                def turn_hidden(t):
                    past(pe, "e_act", k * 4 + t + 1)
                    past(pe, "actT_ready", k * 4 + t)
                    if t == 0:
                        past(pe, "acc_done", k * 4)
                    for b, w in enumerate(bank_columns(nb, m, WIDTHS[t])):
                        for i in range(w // P):
                            ins = turn(ps[6 + b][:, P * i:P * i + P], sg[:, b, P * i:P * i + P], ident[:, :])
                    ins.then_inc(s["e_turned"], 1)

                def output(t):
                    past(pe, "actT_ready", k * 4 + t + 1)
                    n = WIDTHS[t] // per // P
                    w = D // parts
                    if t == 0:
                        past(pe, "y_low", k)
                        past(pe, "y_high", k)
                        past(pe, "acc_done", k * 4)
                    for row in range(parts * n):
                        q, i = row // n, row % n
                        if row % 4 == 0:
                            wd = slot(expert_tile("d", t, row // 4), 4, D)
                        for b in range(nb):
                            for h in range(parts):
                                ins = mm(ps[4 + b // per][m * h:m * h + m, w * (b % per):w * (b % per) + w],
                                         actT[:, t % 2, b // per, n * (b % per) + i, m * q:m * q + m],
                                         wd[:, row % 4, w * h:w * h + w],
                                         start=t == 0 and row == 0 and b % per == 0, stop=t == 3 and row == parts * n - 1,
                                         skip_group_check=per > 1)
                        if row % 4 == 3:
                            ins.then_inc(s["tile_used"], 1)
                past(pe, "hg_ready", g + 1)
                for t in range(4):
                    past(pe, "e_silu", k * 4 + t)
                    hidden("g", t, 0)
                    if t:
                        turn_hidden(t - 1)
                    past(pe, "e_act", k * 4 + t)
                    if t == 0:
                        past(pe, "gT_ready", g + 1)
                    hidden("u", t, 2)
                    if t:
                        output(t - 1)
                turn_hidden(3)
                gather(g + 1, k + 1)
                output(3)
                past(pe, "y_low", k + 1)
                past(pe, "y_high", k + 1)
                for i in range(4):
                    mm(ps[SCATTER[i]][:, :], gcur[0:m * nb, P * (i // 2):P * (i // 2) + P],
                       y_sb[0:m * nb, HALF * (i % 2):HALF * (i % 2) + HALF], start=True, stop=True).then_inc(s["scat_mm"], 1)
            stay_warm(WARM_GATHER, 3)
            pe.wait_ge(s["grow_ready"], 8)

            def first():
                gather(0, 0)
                stay_warm(WARM_ITEM, 2)
            items_loop(pe, "pe", first, item, lambda g, k: gather(g + 1, k))


_INS = ["x", "c", "ada_w", "ada_b", "norm_g", "mix_w_in", "pool_w", "pool_scale", "s5_lam_re", "s5_lam_im",
        "s5_log_step", "s5_b_re", "s5_b_im", "s5_c_re", "s5_c_im", "s5_d", "s5_w_glu", "mix_w_out",
        "ffn_w_gate", "ffn_w_up", "ffn_w_down", "m2_w_in", "m2_conv_w", "m2_conv_b", "m2_dt_bias", "m2_a_log",
        "m2_d", "m2_norm_g", "m2_w_out", "moe_w_router", "moe_b_router", "moe_w_gate", "moe_w_up", "moe_w_down"]


def kernel(**inputs):
    import numpy as _np
    import concourse.bacc as _bacc
    from concourse import mybir as _mybir
    from concourse.bass_utils import run_bass_kernel_spmd as _run

    nc = _bacc.Bacc("TRN2", target_bir_lowering=False, num_devices=1)
    arrays, aps = {}, {}
    for name in _INS:
        v = _np.ascontiguousarray(inputs[name])
        arrays[f"in_{name}"] = v
        aps[name] = nc.dram_tensor(f"in_{name}", v.shape, _mybir.dt.from_np(v.dtype), kind="ExternalInput").ap()
    out = nc.dram_tensor("out", (1, TOK, D), F32, kind="ExternalOutput").ap()
    hybrid_trunk(nc, aps, out)
    r = _run(nc, [arrays], core_ids=[0])
    return r.results[0]["out"]
```
